# Optimizing a Trainium2 kernel written in Bass

```python
import jax, jax.numpy as jnp
from jax import lax
import numpy as np

D_MODEL = 1024
BATCH = 1
SEQ = 1024
DEPTH = 1
DEC_BATCH = 1
DEC_SEQ = 32
PAST_LEN = 256

CHUNK = 64
GLA_HEADS = 4
GLA_DK = 128
GLA_DV = 128
GLA_RANK = 16
GLA_TAU = 16.0
SWA_HEADS = 8
SWA_KV_HEADS = 2
SWA_GROUP = SWA_HEADS // SWA_KV_HEADS
SWA_HD = 64
WINDOW = 128
SWA_BAND = WINDOW // CHUNK
ROPE_DIM = SWA_HD // 4
ROPE_THETA = 500000.0
MEM_TOKENS = 256
MEM_HEADS = 4
MEM_HD = 128
D_FF = 2816
CONV_W = 3
N_BRANCH = 3
ALPHA = (2 * DEPTH) ** 0.25
BETA = (8 * DEPTH) ** -0.25
LN_EPS = 1e-5

IN_SIZES = (GLA_HEADS * GLA_DK, GLA_HEADS * GLA_DK, GLA_HEADS * GLA_DV, GLA_HEADS * GLA_DV, GLA_RANK,
            SWA_HEADS * SWA_HD, SWA_KV_HEADS * SWA_HD, SWA_KV_HEADS * SWA_HD,
            MEM_HEADS * MEM_HD, N_BRANCH * D_MODEL)
IN_COLS = sum(IN_SIZES)
SPLIT_AT = tuple(int(c) for c in np.cumsum(IN_SIZES)[:-1])

kernel_name = "hybrid_gla_swa_mem_convffn_step"

def layer_norm(x, g, b):
    xf = x.astype(jnp.float32)
    mu = jnp.mean(xf, axis=-1, keepdims=True)
    var = jnp.mean(jnp.square(xf - mu), axis=-1, keepdims=True)
    return ((xf - mu) * lax.rsqrt(var + LN_EPS) * g + b).astype(x.dtype)

def rms_norm(x, g):
    xf = x.astype(jnp.float32)
    return (xf * lax.rsqrt(jnp.mean(xf * xf, axis=-1, keepdims=True) + LN_EPS) * g).astype(x.dtype)

def partial_rope(x, pos):
    half = ROPE_DIM // 2
    inv = ROPE_THETA ** (-jnp.arange(half, dtype=jnp.float32) / half)
    ang = pos.astype(jnp.float32)[:, None] * inv[None, :]
    cos, sin = jnp.cos(ang)[:, None, :], jnp.sin(ang)[:, None, :]
    xr = x[..., :ROPE_DIM].astype(jnp.float32)
    x1, x2 = xr[..., :half], xr[..., half:]
    rot = jnp.concatenate([x1 * cos - x2 * sin, x2 * cos + x1 * sin], axis=-1).astype(x.dtype)
    return jnp.concatenate([rot, x[..., ROPE_DIM:]], axis=-1)

def gla_chunked(q, k, v, log_a, s0, block):
    B, T, H, DK = q.shape
    DV = v.shape[-1]
    n = T // block
    f32 = jnp.float32
    qc = q.reshape(B, n, block, H, DK).astype(f32)
    kc = k.reshape(B, n, block, H, DK).astype(f32)
    vc = v.reshape(B, n, block, H, DV).astype(f32)
    b = jnp.cumsum(log_a.reshape(B, n, block, H, DK).astype(f32), axis=2)
    b_last = b[:, :, -1:]
    q_dec = qc * jnp.exp(b)
    k_inv = kc * jnp.exp(-b)
    k_tail = kc * jnp.exp(b_last - b)
    causal = jnp.tril(jnp.ones((block, block), dtype=bool))
    att = jnp.where(causal, jnp.einsum("bnthk,bnshk->bnhts", q_dec, k_inv), 0.0)
    o_intra = jnp.einsum("bnhts,bnshv->bnthv", att, vc)
    ds = jnp.einsum("bnshk,bnshv->bnhkv", k_tail, vc)
    decay = jnp.exp(b_last[:, :, 0])

    def step(S, inp):
        d, dS = inp
        return S * d[..., None] + dS, S

    s_final, s_prev = lax.scan(step, s0.astype(f32), (jnp.moveaxis(decay, 1, 0), jnp.moveaxis(ds, 1, 0)))
    s_prev = jnp.moveaxis(s_prev, 0, 1)
    o_inter = jnp.einsum("bnthk,bnhkv->bnthv", q_dec, s_prev)
    o = (o_intra + o_inter).reshape(B, T, H, DV)
    return o.astype(q.dtype), s_final.astype(s0.dtype)

def sink_softmax(s, sinks):
    sk = sinks.astype(jnp.float32).reshape(SWA_KV_HEADS, SWA_GROUP, 1, 1)
    m = jnp.maximum(jnp.max(s, axis=-1, keepdims=True), sk)
    p = jnp.exp(s - m)
    return p / (jnp.sum(p, axis=-1, keepdims=True) + jnp.exp(sk - m))

def swa_banded(q, k, v, sinks):
    B, T = q.shape[:2]
    n = T // CHUNK
    nb = SWA_BAND + 1
    f32 = jnp.float32
    qc = q.reshape(B, n, CHUNK, SWA_KV_HEADS, SWA_GROUP, SWA_HD).astype(f32)
    pad = ((0, 0), (SWA_BAND * CHUNK, 0), (0, 0), (0, 0))
    kp = jnp.pad(k, pad).reshape(B, n + SWA_BAND, CHUNK, SWA_KV_HEADS, SWA_HD)
    vp = jnp.pad(v, pad).reshape(B, n + SWA_BAND, CHUNK, SWA_KV_HEADS, SWA_HD)
    kb = jnp.concatenate([kp[:, j:j + n] for j in range(nb)], axis=2).astype(f32)
    vb = jnp.concatenate([vp[:, j:j + n] for j in range(nb)], axis=2).astype(f32)
    key_chunk = jnp.arange(n)[:, None] + jnp.arange(nb)[None, :] - SWA_BAND
    valid = jnp.repeat(key_chunk >= 0, CHUNK, axis=1)
    s = jnp.einsum("bnqhgd,bnkhd->bnhgqk", qc, kb) * SWA_HD ** -0.5
    s = jnp.where(valid[None, :, None, None, None, :], s, -jnp.inf)
    p = sink_softmax(s, sinks)
    o = jnp.einsum("bnhgqk,bnkhd->bnqhgd", p, vb)
    return o.reshape(B, T, SWA_HEADS * SWA_HD).astype(q.dtype)

def swa_with_history(q, k_all, v_all, sinks):
    B, T = q.shape[:2]
    f32 = jnp.float32
    qg = q.reshape(B, T, SWA_KV_HEADS, SWA_GROUP, SWA_HD).astype(f32)
    s = jnp.einsum("bqhgd,bkhd->bhgqk", qg, k_all.astype(f32)) * SWA_HD ** -0.5
    p = sink_softmax(s, sinks)
    o = jnp.einsum("bhgqk,bkhd->bqhgd", p, v_all.astype(f32))
    return o.reshape(B, T, SWA_HEADS * SWA_HD).astype(q.dtype)

def mem_attention(q, mk, mv):
    B, T = q.shape[:2]
    s = jnp.einsum("bthd,bmhd->bhtm", q.astype(jnp.float32), mk.astype(jnp.float32)) * MEM_HD ** -0.5
    p = jax.nn.softmax(s, axis=-1)
    o = jnp.einsum("bhtm,bmhd->bthd", p, mv.astype(jnp.float32))
    return o.reshape(B, T, MEM_HEADS * MEM_HD).astype(q.dtype)

def conv_ffn(x, hist, w_up, conv_w, conv_b, w_down):
    T = x.shape[1]
    u = x @ w_up
    ue = jnp.concatenate([hist.astype(u.dtype), u], axis=1)
    c = conv_b + sum(ue[:, j:j + T] * conv_w[j] for j in range(CONV_W))
    gate, val = jnp.split(c, 2, axis=-1)
    return (jax.nn.gelu(gate) * val) @ w_down, ue[:, -(CONV_W - 1):]

def _layer(x, pos, gla_s0, swa_k_hist, swa_v_hist, mem_k, mem_v, conv_hist, w):
    B, T, _ = x.shape
    z = x @ w["w_in"]
    gq, gk, gv, gr, ga, sq, sk, sv, mq, gl = jnp.split(z, SPLIT_AT, axis=-1)
    log_a = jax.nn.log_sigmoid((ga @ w["w_gla_a2"] + w["b_gla_a"]).astype(jnp.float32)) / GLA_TAU
    o_a, gla_s = gla_chunked(gq.reshape(B, T, GLA_HEADS, GLA_DK) * GLA_DK ** -0.5,
                             gk.reshape(B, T, GLA_HEADS, GLA_DK),
                             gv.reshape(B, T, GLA_HEADS, GLA_DV),
                             log_a.reshape(B, T, GLA_HEADS, GLA_DK), gla_s0, min(CHUNK, T))
    o_a = rms_norm(o_a, w["gla_norm_g"]) * jax.nn.silu(gr.reshape(B, T, GLA_HEADS, GLA_DV))
    y_a = o_a.reshape(B, T, GLA_HEADS * GLA_DV) @ w["w_br_gla"]
    q = partial_rope(sq.reshape(B, T, SWA_HEADS, SWA_HD), pos)
    k = partial_rope(sk.reshape(B, T, SWA_KV_HEADS, SWA_HD), pos)
    v = sv.reshape(B, T, SWA_KV_HEADS, SWA_HD)
    if swa_k_hist is None:
        o_b = swa_banded(q, k, v, w["swa_sinks"])
        k_all, v_all = k, v
    else:
        k_all = jnp.concatenate([swa_k_hist.astype(k.dtype), k], axis=1)
        v_all = jnp.concatenate([swa_v_hist.astype(v.dtype), v], axis=1)
        o_b = swa_with_history(q, k_all, v_all, w["swa_sinks"])
    y_b = o_b @ w["w_br_swa"]
    o_c = mem_attention(mq.reshape(B, T, MEM_HEADS, MEM_HD), mem_k, mem_v)
    y_c = o_c @ w["w_br_mem"]
    g_a, g_b, g_c = jnp.split(jax.nn.sigmoid(gl + w["b_gate"]), N_BRANCH, axis=-1)
    mix = (g_a * y_a + g_b * y_b + g_c * y_c) @ w["w_o"]
    x = layer_norm(ALPHA * x + mix, w["ln1_g"], w["ln1_b"])
    f, conv_new = conv_ffn(x, conv_hist, w["w_up"], w["conv_w"], w["conv_b"], w["w_down"])
    x = layer_norm(ALPHA * x + f, w["ln2_g"], w["ln2_b"])
    return x, gla_s, k_all[:, -WINDOW:], v_all[:, -WINDOW:], conv_new

def setup_inputs(seed: int = 0) -> dict:
    key = jax.random.key(seed)
    ks = iter(jax.random.split(key, 32))

    def nrm(shape, scale):
        return jax.random.normal(next(ks), shape, jnp.float32) * scale

    L, D, F = DEPTH, D_MODEL, D_FF
    return {
        "x_prompt": nrm((BATCH, SEQ, D), 1.0),
        "x_sample": nrm((DEC_BATCH, DEC_SEQ, D), 1.0),
        "cache_swa_k": nrm((L, DEC_BATCH, WINDOW, SWA_KV_HEADS, SWA_HD), 1.0),
        "cache_swa_v": nrm((L, DEC_BATCH, WINDOW, SWA_KV_HEADS, SWA_HD), 1.0),
        "state_gla": nrm((L, DEC_BATCH, GLA_HEADS, GLA_DK, GLA_DV), 1.0),
        "cache_mem_k": nrm((L, DEC_BATCH, MEM_TOKENS, MEM_HEADS, MEM_HD), 1.0),
        "cache_mem_v": nrm((L, DEC_BATCH, MEM_TOKENS, MEM_HEADS, MEM_HD), 1.0),
        "cache_ffn_conv": nrm((L, DEC_BATCH, CONV_W - 1, 2 * F), 1.0),
        "mem_prompt": nrm((BATCH, MEM_TOKENS, D), 1.0),
        "ln1_g": 1.0 + nrm((L, D), 0.02),
        "ln1_b": nrm((L, D), 0.02),
        "ln2_g": 1.0 + nrm((L, D), 0.02),
        "ln2_b": nrm((L, D), 0.02),
        "w_in": nrm((L, D, IN_COLS), D ** -0.5),
        "b_gate": nrm((L, N_BRANCH * D), 0.02),
        "w_gla_a2": nrm((L, GLA_RANK, GLA_HEADS * GLA_DK), GLA_RANK ** -0.5),
        "b_gla_a": nrm((L, GLA_HEADS * GLA_DK), 0.1),
        "gla_norm_g": 1.0 + nrm((L, GLA_DV), 0.02),
        "swa_sinks": nrm((L, SWA_HEADS), 0.5),
        "w_mem_kv": nrm((L, D, 2 * MEM_HEADS * MEM_HD), D ** -0.5),
        "w_br_gla": nrm((L, GLA_HEADS * GLA_DV, D), (GLA_HEADS * GLA_DV) ** -0.5),
        "w_br_swa": nrm((L, SWA_HEADS * SWA_HD, D), (SWA_HEADS * SWA_HD) ** -0.5),
        "w_br_mem": nrm((L, MEM_HEADS * MEM_HD, D), (MEM_HEADS * MEM_HD) ** -0.5),
        "w_o": nrm((L, D, D), D ** -0.5 * BETA),
        "w_up": nrm((L, D, 2 * F), D ** -0.5),
        "conv_w": nrm((L, CONV_W, 2 * F), CONV_W ** -0.5),
        "conv_b": nrm((L, 2 * F), 0.02),
        "w_down": nrm((L, F, D), F ** -0.5 * BETA),
    }

def reference(x_prompt, x_sample, cache_swa_k, cache_swa_v, state_gla, cache_mem_k, cache_mem_v,
              cache_ffn_conv, mem_prompt, ln1_g, ln1_b, ln2_g, ln2_b, w_in, b_gate, w_gla_a2, b_gla_a,
              gla_norm_g, swa_sinks, w_mem_kv, w_br_gla, w_br_swa, w_br_mem, w_o, w_up, conv_w, conv_b,
              w_down):
    Bp, Tp, _ = x_prompt.shape
    Bs, Ts, _ = x_sample.shape
    pos_p = jnp.arange(Tp, dtype=jnp.int32)
    pos_s = PAST_LEN + jnp.arange(Ts, dtype=jnp.int32)
    hp, hs = x_prompt, x_sample
    p_swk, p_swv, p_gla, p_mk, p_mv, p_conv = [], [], [], [], [], []
    s_swk, s_swv, s_gla, s_conv = [], [], [], []
    for l in range(DEPTH):
        w = dict(ln1_g=ln1_g[l], ln1_b=ln1_b[l], ln2_g=ln2_g[l], ln2_b=ln2_b[l], w_in=w_in[l],
                 b_gate=b_gate[l], w_gla_a2=w_gla_a2[l], b_gla_a=b_gla_a[l], gla_norm_g=gla_norm_g[l],
                 swa_sinks=swa_sinks[l], w_br_gla=w_br_gla[l], w_br_swa=w_br_swa[l], w_br_mem=w_br_mem[l],
                 w_o=w_o[l], w_up=w_up[l], conv_w=conv_w[l], conv_b=conv_b[l], w_down=w_down[l])
        mk_p, mv_p = [t.reshape(Bp, MEM_TOKENS, MEM_HEADS, MEM_HD)
                      for t in jnp.split(mem_prompt @ w_mem_kv[l], 2, axis=-1)]
        gla0 = jnp.zeros((Bp, GLA_HEADS, GLA_DK, GLA_DV), x_prompt.dtype)
        conv0 = jnp.zeros((Bp, CONV_W - 1, 2 * D_FF), x_prompt.dtype)
        hp, g_p, k_p, v_p, c_p = _layer(hp, pos_p, gla0, None, None, mk_p, mv_p, conv0, w)
        hs, g_s, k_s, v_s, c_s = _layer(hs, pos_s, state_gla[l], cache_swa_k[l], cache_swa_v[l],
                                        cache_mem_k[l], cache_mem_v[l], cache_ffn_conv[l], w)
        p_swk.append(k_p); p_swv.append(v_p); p_gla.append(g_p)
        p_mk.append(mk_p); p_mv.append(mv_p); p_conv.append(c_p)
        s_swk.append(k_s); s_swv.append(v_s); s_gla.append(g_s); s_conv.append(c_s)
    return (hp, hs,
            jnp.stack(p_swk), jnp.stack(p_swv), jnp.stack(p_gla), jnp.stack(p_mk), jnp.stack(p_mv),
            jnp.stack(p_conv),
            jnp.stack(s_swk), jnp.stack(s_swv), jnp.stack(s_gla), jnp.stack(s_conv))


_drawn_inputs = setup_inputs


def setup_inputs(seed=0):
    import zlib

    import numpy as np

    out = dict(_drawn_inputs(seed))
    spreads = {}
    factors = {'ln1_g': 2.713,
     'ln1_b': 2.78,
     'ln2_g': 22.515,
     'ln2_b': 23.098,
     'b_gate': 8.0,
     'gla_norm_g': 24.195,
     'swa_sinks': 200.0,
     'conv_b': 6.538,
     'cache_mem_k': 3.519,
     'w_br_swa': 8.0}
    for name, (base, spread) in spreads.items():
        noise = np.random.default_rng([zlib.crc32(name.encode()), seed]).standard_normal(out[name].shape)
        drawn = base * np.exp(spread * noise) if base else spread * noise
        out[name] = __import__('jax').numpy.asarray(drawn.astype(out[name].dtype))
    for name, factor in factors.items():
        out[name] = (out[name] * factor).astype(out[name].dtype)
    return out
```

```python
from contextlib import ExitStack

import numpy as np

import concourse.bass as bass
from concourse import mybir

F32 = mybir.dt.float32
F32R = mybir.dt.float32r
I32 = mybir.dt.int32
ALU = mybir.AluOpType
ACT = mybir.ActivationFunctionType
AX_X = mybir.AxisListType.X

P = 128
D = 1024
KD = D // P
SEQ, DEC = 1024, 32
GAP = 2
SAMPLE = SEQ + GAP
TT = SAMPLE + DEC
GROUPS = ((0, 352), (352, 352), (704, TT - 704))
GW = GROUPS[2][1]
NT = SEQ // P
H = 4
BLK = 64
RANK = 16
DFF = 2816
NF = DFF // P
MEM = 256
PAST = 256
ROPE_DIM, ROPE_THETA, SWA_HD = 16, 500000.0, 64
ALPHA = 2.0 ** 0.25
LN_EPS = 1e-5
GLA_TAU = 16.0
GLA_SCALE = 128.0 ** -0.5
SWA_SCALE = 64.0 ** -0.5
MEM_SCALE = 128.0 ** -0.5
NEG = -1.0e30

C_GQ, C_GK, C_GV, C_GR, C_GA = 0, 512, 1024, 1536, 2048
C_SQ, C_SK, C_SV, C_MQ, C_GL = 2064, 2576, 2704, 2832, 3344
IN_COLS = 6416

T_GLA = 0
T_GATE_A = 16
T_ATT = 32
T_MEM = 42
T_GATE_B = 50
T_MERGE = 58
T_WO = 70
T_FFN = 78

PW0, PW1, PBG, PW2, PCB, PGN, PHI = 0, NF * 2, NF * 4, NF * 4 + 24, NF * 6 + 24, NF * 8 + 24, NF * 8 + 25
NPRM = PHI + NF * 4


def shape_constants():
    ident = np.eye(P, dtype=np.float32)
    s, t = np.meshgrid(np.arange(P), np.arange(P), indexing="ij")
    causal = (s <= t) & (s // BLK == t // BLK)
    cumsum = (causal / GLA_TAU).astype(np.float32)
    q, k = np.meshgrid(np.arange(P), np.arange(2 * P), indexing="ij")
    band = ((q < 64) & (k < 192)) | ((q >= 64) & (k >= 64))
    mask = np.where(band, 0.0, NEG).astype(np.float32)
    mask_first = np.where(band & (k >= P), 0.0, NEG).astype(np.float32)
    half = ROPE_DIM // 2
    turn = np.zeros((P, P), np.float32)
    for base in (0, SWA_HD):
        for d in range(half):
            turn[base + d + half, base + d] = -1.0
            turn[base + d, base + d + half] = 1.0
    inv = np.float32(ROPE_THETA) ** (-np.arange(half, dtype=np.float32) / np.float32(half))
    pos = np.concatenate([np.arange(SEQ), np.zeros(GAP), PAST + np.arange(DEC)]).astype(np.float32)
    ang = pos[None, :] * inv.astype(np.float32)[:, None]
    cos = np.ones((P, TT), np.float32)
    sin = np.zeros((P, TT), np.float32)
    for base in (0, SWA_HD):
        for h in (0, half):
            cos[base + h:base + h + half] = np.cos(ang)
            sin[base + h:base + h + half] = np.sin(ang)
    return {"c_ident": ident, "c_cumsum": cumsum, "c_causal": causal.astype(np.int32), "c_mask": mask,
            "c_mask_first": mask_first, "c_turn": turn, "c_cos": cos, "c_sin": sin}


def align(address):
    return (address + 31) // 32 * 32


class Arena:

    def __init__(self, nc, base, size):
        self.nc, self.at, self.end = nc, base, base + size

    def take(self, name, shape, dtype):
        size = int(np.prod(shape[1:])) * 4
        t = self.nc.alloc_sbuf_tensor_at(name, shape, dtype, offset=self.at)
        self.at += align(size)
        assert self.at <= self.end, (name, self.at - self.end)
        return t


class Semaphores:

    def __init__(self, sem):
        self.w_split_hi, self.w_split_lo = map(sem, ("w_split_hi", "w_split_lo"))
        self.consts, self.params, self.gla_consts = map(sem, ("consts", "params", "gla_consts"))
        self.att_consts, self.mem_in, self.ln_consts = map(sem, ("att_consts", "mem_in", "ln_consts"))
        self.sample_in, self.state_in = map(sem, ("sample_in", "state_in"))
        self.zeroed, self.prm_turned, self.prm_ready = map(sem, ("zeroed", "prm_turned", "prm_ready"))
        self.x_turned, self.x_hi_done, self.x_lo_done = map(sem, ("x_turned", "x_hi_done", "x_lo_done"))
        self.wga_split_hi, self.wga_ready = map(sem, ("wga_split_hi", "wga_ready"))
        self.proj_done, self.proj_free = map(sem, ("proj_done", "proj_free"))
        self.ga_staged, self.v_staged, self.la_mm = map(sem, ("ga_staged", "v_staged", "la_mm"))
        self.abs_done, self.expabs_done, self.ln1p_done = map(sem, ("abs_done", "expabs_done", "ln1p_done"))
        self.la_ready, self.b_mm, self.b_copied = map(sem, ("la_ready", "b_mm", "b_copied"))
        self.epos_ready, self.eneg_ready, self.decay_ready = map(sem, ("epos_ready", "eneg_ready", "decay_ready"))
        self.diff_ready, self.etail_ready, self.qdec_ready = map(sem, ("diff_ready", "etail_ready", "qdec_ready"))
        self.kinv_ready, self.ktail_ready, self.v_turned = map(sem, ("kinv_ready", "ktail_ready", "v_turned"))
        self.vtok_ready, self.kt_turned, self.kttok_ready = map(sem, ("vtok_ready", "kt_turned", "kttok_ready"))
        self.att_ready, self.dsa_mm, self.state_mid, self.o_mm = map(sem, ("att_ready", "dsa_mm", "state_mid", "o_mm"))
        self.dsb_mm, self.state_end, self.osq_ready = map(sem, ("dsb_mm", "state_end", "osq_ready"))
        self.rms_mm, self.lnms_done, self.rstd_ready = map(sem, ("rms_mm", "lnms_done", "rstd_ready"))
        self.er_ready, self.er1_ready, self.erec_ready = map(sem, ("er_ready", "er1_ready", "erec_ready"))
        self.silu_ready, self.o_normed, self.gla_out = map(sem, ("silu_ready", "o_normed", "gla_out"))
        self.rope_mm, self.rope_sin, self.rope_cos = map(sem, ("rope_mm", "rope_sin", "rope_cos"))
        self.rope_done, self.mem_turned, self.mem_hi_done = map(sem, ("rope_done", "mem_turned", "mem_hi_done"))
        self.mem_lo_done, self.mk_turned, self.mk_ready = map(sem, ("mem_lo_done", "mk_turned", "mk_ready"))
        self.staged, self.vs_turned, self.vt_ready = map(sem, ("staged", "vs_turned", "vt_ready"))
        self.scores_mm, self.masked, self.max_done = map(sem, ("scores_mm", "masked", "max_done"))
        self.nbias_done, self.sdif_done, self.sexp_done = map(sem, ("nbias_done", "sdif_done", "sexp_done"))
        self.exp_done, self.den_done, self.rec_done = map(sem, ("exp_done", "den_done", "rec_done"))
        self.prob_ready, self.prob_turned, self.pT_dve = map(sem, ("prob_ready", "prob_turned", "pT_dve"))
        self.pT_act, self.pv_mm, self.o_evac, self.k_turned = map(sem, ("pT_act", "pv_mm", "o_evac", "k_turned"))
        self.k_out_ready, self.sample_turned = map(sem, ("k_out_ready", "sample_turned"))
        self.sample_ready, self.v_out_ready = map(sem, ("sample_ready", "v_out_ready"))
        self.oh_split, self.ol_split, self.y_mm, self.part_done = map(sem, ("oh_split", "ol_split", "y_mm", "part_done"))
        self.acc_add, self.acc_ready, self.mix_hi_done = map(sem, ("acc_add", "acc_ready", "mix_hi_done"))
        self.mix_ready, self.gate_sig = map(sem, ("mix_ready", "gate_sig"))
        self.wo_mm, self.wo_free, self.r_turned, self.r_done = map(sem, ("wo_mm", "wo_free", "r_turned", "r_done"))
        self.stats_done, self.aggr_done, self.sd_done = map(sem, ("stats_done", "aggr_done", "sd_done"))
        self.rs_done, self.nm_done, self.norm_done, self.scaled = map(sem, ("rs_done", "nm_done", "norm_done", "scaled"))
        self.shifted, self.x1_turned, self.x1_lo_done = map(sem, ("shifted", "x1_turned", "x1_lo_done"))
        self.x1_acc_done = sem("x1_acc_done")
        self.u_zeroed, self.up_mm, self.u_hist, self.u_tail = map(sem, ("u_zeroed", "up_mm", "u_hist", "u_tail"))
        self.conv_part, self.conv_done, self.gelu_done = map(sem, ("conv_part", "conv_done", "gelu_done"))
        self.hmul_done, self.h_hi_done, self.h_ready = map(sem, ("hmul_done", "h_hi_done", "h_ready"))
        self.down_mm, self.down_free, self.up_done = map(sem, ("down_mm", "down_free", "up_done"))
        self.mem_used, self.cleared, self.tails_turned = map(sem, ("mem_used", "cleared", "tails_turned"))
        self.tails_ready = sem("tails_ready")
        self.st_state, self.st_memk, self.st_memv, self.stored = map(sem, ("st_state", "st_memk", "st_memv", "stored"))


def build(nc, I, O):
    with ExitStack() as ctx:
        program(nc, I, O, ctx)


def program(nc, I, O, ctx):
    sem = lambda name: ctx.enter_context(nc.semaphore(name))

    X_BYTES, Z_BYTES, B_BYTES, RING_BYTES = 2 * KD * TT * 4, 16 * TT * 4, 12 * TT * 4, 6 * 4096
    X_AT = align(nc.sbuf_base)
    Z_AT = X_AT + X_BYTES
    B_AT = Z_AT + Z_BYTES
    R_AT = B_AT + B_BYTES
    S_AT = R_AT + RING_BYTES
    at = nc.alloc_sbuf_tensor_at
    act_hi = at("act_hi", [P, KD, TT], F32R, offset=X_AT)
    act_lo = at("act_lo", [P, KD, TT], F32R, offset=X_AT + KD * TT * 4)
    mix_acc = at("mix_acc", [P, KD, TT], F32, offset=X_AT + KD * TT * 4)
    z = at("z", [P, 16, TT], F32, offset=Z_AT)
    z_lo = at("z_lo", [P, 16, TT], F32R, offset=Z_AT)
    o_hi = at("o_hi", [P, 12, TT], F32R, offset=B_AT)
    acc = at("acc", [P, KD, TT], F32, offset=B_AT)
    ring = Arena(nc, R_AT, RING_BYTES)
    w_raw = [ring.take(f"w_raw{i}", [P, KD, P], F32) for i in range(2)]
    w_hi = [ring.take(f"w_hi{i}", [P, KD, P], F32R) for i in range(2)]
    w_lo = [ring.take(f"w_lo{i}", [P, KD, P], F32R) for i in range(2)]
    small = Arena(nc, S_AT, nc.sbuf_usable_end - S_AT)
    ident = small.take("ident", [P, P], F32)
    prm = small.take("prm", [P, NPRM], F32)
    sink = small.take("sink", [P, 8], F32)
    neg_sink = small.take("neg_sink", [P, 8], F32)
    eps = small.take("eps", [P, 1], F32)

    X0 = 9 * D * 4
    x_rows = at("x_rows", [P, 9, D], F32, offset=B_AT)
    up0 = Arena(nc, B_AT + X0, B_BYTES - X0)
    wa2 = up0.take("wa2", [33, 512], F32)
    cumsum = up0.take("cumsum", [P, P], F32)
    causal = up0.take("causal", [P, P], I32)
    wga = up0.take("wga", [P, KD, RANK], F32)
    wga_hi = up0.take("wga_hi", [P, KD, RANK], F32R)
    wga_lo = up0.take("wga_lo", [P, KD, RANK], F32R)
    ones = up0.take("ones", [P, P], F32)
    ga_T = up0.take("ga_T", [33, TT], F32)
    S_a = up0.take("S_a", [P, H, P], F32)
    S_b = up0.take("S_b", [P, H, P], F32)
    prow = [at(f"prow{i}", [P, P], F32, offset=Z_AT + 512 * i) for i in range(3)]
    g = Arena(nc, B_AT, X0)
    ga_s = g.take("ga_s", [33, P], F32)
    sp_a = g.take("sp_a", [P, 512], F32)
    sp_l = g.take("sp_l", [P, 512], F32)
    la = g.take("la", [P, 512], F32)
    b_s = g.take("b_s", [P, H, P], F32)
    e_p = g.take("e_p", [P, H, P], F32)
    e_n = g.take("e_n", [P, H, P], F32)
    e_t = g.take("e_t", [P, H, P], F32)
    q_dec = g.take("q_dec", [P, H, P], F32)
    k_inv = g.take("k_inv", [P, H, P], F32)
    k_tail = g.take("k_tail", [P, H, P], F32)
    v_s = g.take("v_s", [P, H, P], F32)
    v_tok = g.take("v_tok", [P, H, P], F32)
    kt_tok = g.take("kt_tok", [P, H, P], F32)
    att = g.take("att", [P, H, P], F32)
    silu = g.take("silu", [P, H, P], F32)
    gate_st = [g.take(f"gate_st{i}", [P, GW], F32) for i in range(3)]
    decay = g.take("decay", [P, H, 2], F32)
    osq4, rstd4, lnms4 = (x[:, :].rearrange("p (h c) -> p h c", h=H) for x in (sp_a, sp_l, la))
    er = b_s
    m = Arena(nc, B_AT, B_BYTES)
    mkT = [m.take("mkT_p", [P, H, MEM], F32)]
    mv = [m.take("mv_p", [P, 2, 512], F32)]
    mask = m.take("mask", [P, 2 * P], F32)
    mask_first = m.take("mask_first", [P, 2 * P], F32)
    FREE_AT = m.at
    mem_hi = m.take("mem_hi", [P, KD, MEM], F32R)
    mem_lo = m.take("mem_lo", [P, KD, MEM], F32R)
    mem_rows = [m.take(f"mem_rows{i}", [P, D], F32) for i in range(2)]
    mk_rows = at("mk_rows", [P, 2, 512], F32, offset=B_AT + B_BYTES - 4096)
    turn = m.take("turn", [P, P], F32)
    rope_t = [m.take(f"rope_t{i}", [P, GW], F32) for i in range(2)]
    cos = m.take("cos", [P, TT], F32)
    sin = m.take("sin", [P, TT], F32)
    kpad = at("kpad", [P, P + TT], F32, offset=align(Z_AT + 10 * TT * 4))
    a = Arena(nc, FREE_AT, B_AT + B_BYTES - FREE_AT)
    qs = [a.take(f"qs{i}", [P, H, P], F32) for i in range(2)]
    mqs = [a.take(f"mqs{i}", [P, H, P], F32) for i in range(2)]
    ks = [a.take(f"ks{i}", [P, 2 * P], F32) for i in range(2)]
    vs = [a.take(f"vs{i}", [P, P], F32) for i in range(2)]
    vt = [a.take(f"vt{i}", [P, P], F32) for i in range(2)]
    prob = [a.take(f"prob{i}", [P, H, 2 * P], F32) for i in range(2)]
    prob_T = a.take("prob_T", [P, 2 * H, P], F32)
    gate_st2 = [a.take(f"gate_stb{i}", [P, GW], F32) for i in range(3)]
    smax = [a.take(f"smax{i}", [P, H], F32) for i in range(2)]
    nbias = [a.take(f"nbias{i}", [P, H], F32) for i in range(2)]
    ssum = [a.take(f"ssum{i}", [P, H], F32) for i in range(2)]
    sdif = [a.take(f"sdif{i}", [P, H], F32) for i in range(2)]
    sexp = [a.take(f"sexp{i}", [P, H], F32) for i in range(2)]
    sden = [a.take(f"sden{i}", [P, H], F32) for i in range(2)]
    srec = [a.take(f"srec{i}", [P, H], F32) for i in range(2)]
    mkT.append(a.take("mkT_s", [P, H, MEM], F32))
    mv.append(a.take("mv_s", [P, 2, 512], F32))
    v_hist = a.take("v_hist", [P, P], F32)
    k_hist = a.take("k_hist", [P, P], F32)
    ks_s = a.take("ks_s", [P, P + DEC], F32)
    mk_s = at("mk_s", [P, 2, 512], F32, offset=Z_AT + 8 * TT * 4)
    xs = Arena(nc, align(X_AT + (KD - 1) * TT * 4), TT * 4 - 32)
    k_out = xs.take("k_out", [P, P], F32)
    v_out = xs.take("v_out", [P, P], F32)
    k_out_s = xs.take("k_out_s", [DEC, P], F32)
    v_out_s = xs.take("v_out_s", [DEC, P], F32)
    spare = Arena(nc, Z_AT + 8 * TT * 4, 4 * TT * 4)
    gate_in = [spare.take(f"gate_in{i}", [P, TT], F32) for i in range(2)]
    part = [spare.take(f"part{i}", [P, GW], F32) for i in range(4)]
    wo_hi = at("wo_hi", [P, KD, KD, P], F32R, offset=Z_AT)
    wo_lo = at("wo_lo", [P, KD, KD, P], F32R, offset=Z_AT + KD * D * 4)
    n = Arena(nc, B_AT + KD * TT * 4, B_BYTES - KD * TT * 4)
    rows = [n.take(f"rows{i}", [P, D], F32) for i in range(2)]
    ln_g = n.take("ln_g", [P, D], F32)
    ln_b = n.take("ln_b", [P, D], F32)
    ln_st = [n.take(f"ln_st{i}", [P, 2, 6], F32) for i in range(2)]
    ln_mv = [n.take(f"ln_mv{i}", [P, 2], F32) for i in range(2)]
    ln_sd = [n.take(f"ln_sd{i}", [P, 1], F32) for i in range(2)]
    ln_rs = [n.take(f"ln_rs{i}", [P, 1], F32) for i in range(2)]
    ln_nm = [n.take(f"ln_nm{i}", [P, 1], F32) for i in range(2)]
    f = Arena(nc, Z_AT, Z_BYTES)
    w3_hi = f.take("w3_hi", [P, KD, P], F32R)
    w3_lo = f.take("w3_lo", [P, KD, P], F32R)
    U_AT = f.at
    u = [[f.take(f"u{i}{j}", [P, GAP + TT], F32) for j in range(2)] for i in range(2)]
    conv = [f.take(f"conv{j}", [P, TT], F32) for j in range(2)]
    h_hi = [f.take(f"h_hi{j}", [P, TT], F32R) for j in range(2)]
    h_lo = [f.take(f"h_lo{j}", [P, TT], F32R) for j in range(2)]
    tails = f.take("tails", [P, 4, NF * 2], F32)
    tails_T = [f.take(f"tails_T{i}", [88, P], F32) for i in range(2)]
    y_rows = [at(f"y_rows{i}", [P, D], F32, offset=U_AT + 4096 * i) for i in range(4)]

    psum = ctx.enter_context(nc.psum_tensor("banks", [P, 8, 512], F32))
    bank = lambda b: psum[:, b, :]
    bank4 = lambda b: psum[:, b, :].rearrange("p (h c) -> p h c", h=4)
    pair8 = lambda b: psum[:, b:b + 2, :].rearrange("p b (h c) -> p (b h) c", c=P)
    gates = nc.dram_tensor("gates_scratch", (3 * KD, P, TT), F32, kind="Internal").ap()

    w_in = I["w_in"].rearrange("l (k p) c -> p (l k) c", p=P)
    w_kv = I["w_mem_kv"].rearrange("l (k p) c -> p (l k) c", p=P)
    w_up = I["w_up"].rearrange("l (k p) c -> p (l k) c", p=P)
    w_o = I["w_o"].rearrange("l (k p) c -> p (l k) c", p=P)
    w_down = I["w_down"].rearrange("l (f p) c -> p (l f) c", p=P)
    w_br_mem = I["w_br_mem"].rearrange("l (k p) c -> p (l k) c", p=P)
    w_br_gla = I["w_br_gla"].rearrange("l (k p) c -> p (l k) c", p=P)
    w_br_swa = I["w_br_swa"].rearrange("l (g k p) c -> g p (l k) c", g=2, p=64)

    GATE_OF = (1, 2, 0)
    ROPE_CHUNKS = (0, 1, 2, 3, 8)
    PS_GA, PS_GATE_A, PS_ATT, PS_MEM, PS_GATE_B, PS_END = 48, 51, 99, 129, 133, 157
    q = Semaphores(sem)
    w_landed = [sem(f"w_landed{i}") for i in range(2)]
    x_landed = [sem(f"x_landed{i}") for i in range(4)]
    rows_landed = [sem(f"rows_landed{i}") for i in range(2)]
    gate_stored = [sem(f"gate_stored{i}") for i in range(3)]
    gate_landed = [sem(f"gate_landed{i}") for i in range(2)]
    y_stored = [sem(f"y_stored{i}") for i in range(4)]

    X_GROUP = (0, 1, 2, 2, 2, 3, 3, 3, 3)

    def tile_of(turn, slot):
        return turn * 2 + slot

    def tok(t):
        return (SAMPLE, DEC) if isinstance(t, int) and t == NT else (t * P, P)

    block = ctx.enter_context(nc.Block())

    @block.sync
    def _(sp):
        def load(turn, slot, halves):
            if not (isinstance(turn, int) and turn == 0):
                sp.wait_ge(q.w_split_lo, tile_of(turn, slot) - 1)
            for dst, src in halves:
                sp.dma_start(dst, src).then_inc(w_landed[slot], 16)

        def cols(turn, slot, w, c):
            load(turn, slot, [(w_raw[slot][:, 4 * i:4 * i + 4, :], w[:, 4 * i:4 * i + 4, bass.ds(c, P)]) for i in range(2)])

        def swa_q(turn, slot, k):
            load(turn, slot, [(w_raw[slot][:, :, 64 * i:64 * i + 64],
                               w_in[:, :, bass.ds(C_SQ + 256 * i + k * 64, 64)]) for i in range(2)])

        def flat(slot, i, n):
            return w_raw[slot][:, 4 * i:4 * i + 4, :].rearrange("p k c -> p (k c)")

        sp.dma_start(ident[:, :], I["c_ident"]).then_inc(q.consts, 16)
        for t in range(9):
            if t < NT:
                sp.dma_start(x_rows[:, t, :], I["x_prompt"][0, t * P:(t + 1) * P, :]).then_inc(x_landed[X_GROUP[t]], 16)
            else:
                sp.dma_start(x_rows[0:DEC, t, :], I["x_sample"][0]).then_inc(x_landed[X_GROUP[t]], 16)
            if t == 1:
                conv_rows = I["conv_w"].rearrange("l w (j p) -> (l w j) p", p=P)
                sp.dma_start(prow[0][0:88, :], conv_rows[0:88]).then_inc(q.params, 16)
                sp.dma_start(prow[0][88:112, :], I["b_gate"].rearrange("l (j p) -> (l j) p", p=P)).then_inc(q.params, 16)
                sp.dma_start(prow[1][0:44, :], conv_rows[88:132]).then_inc(q.params, 16)
                sp.dma_start(prow[1][44:88, :], I["conv_b"].rearrange("l (j p) -> (l j) p", p=P)).then_inc(q.params, 16)
                sp.dma_start(prow[1][88:89, :], I["gla_norm_g"]).then_inc(q.params, 16)
                sp.dma_start(prow[2][0:88, :], I["cache_ffn_conv"].rearrange("l b w (j p) -> (l b w j) p", p=P)).then_inc(q.params, 16)
                sp.dma_start(sink[:, :], I["swa_sinks"].to_broadcast([P, 8])).then_inc(q.params, 16)
                cols(0, 0, w_in, C_GQ)
            if t == 2:
                cols(0, 1, w_in, C_GQ + P)
        sp.dma_start(cumsum[:, :], I["c_cumsum"]).then_inc(q.gla_consts, 16)
        sp.dma_start(causal[:, :], I["c_causal"]).then_inc(q.gla_consts, 16)
        sp.dma_start(wga[:, :, :], w_in[:, :, C_GA:C_GA + RANK]).then_inc(q.gla_consts, 16)
        sp.wait_ge(q.zeroed, 1)
        sp.dma_start(wa2[0:RANK, :], I["w_gla_a2"][0]).then_inc(q.gla_consts, 16)
        sp.dma_start(wa2[32:33, :], I["b_gla_a"]).then_inc(q.gla_consts, 16)

        with sp.Fori(1, 8) as i:
            for j in range(2):
                cols(i, j, w_in, i * 256 + C_GQ + j * P)

        def gate_loop(turn0, chunk0, n, staging, stored0):
            for j in range(2):
                cols(turn0, j, w_in, C_GL + (chunk0 + j) * P)
            def stores(i):
                for j in range(2):
                    for s, (c, w) in enumerate(GROUPS):
                        sp.wait_ge(q.proj_free, stored0 + i * 6 + 3 * j + s + 1)
                        sp.dma_start(gates[bass.ds(i * 2 + chunk0 + j, 1), :, c:c + w].rearrange("a p c -> p (a c)"),
                                     staging[s][:, 0:w]).then_inc(gate_stored[s], 16)
            with sp.Fori(0, n - 1) as i:
                for j in range(2):
                    cols(i + (turn0 + 1), j, w_in, i * 256 + C_GL + (chunk0 + 2 + j) * P)
                stores(i)
            return stores

        last = gate_loop(T_GATE_A // 2, 0, 8, gate_st, PS_GATE_A)
        for j in range(2):
            swa_q(T_ATT // 2, j, j)
        last(7)
        for j in range(2):
            swa_q(T_ATT // 2 + 1, j, 2 + j)
        sp.wait_ge(q.gla_out, NT + 1)
        sp.wait_ge(q.dsa_mm, NT + 1)
        for s in range(3):
            sp.wait_ge(gate_stored[s], 16 * 16)
        sp.wait_ge(q.st_state, 32)
        sp.dma_start(turn[:, :], I["c_turn"]).then_inc(q.att_consts, 16)
        sp.dma_start(cos[:, :], I["c_cos"]).then_inc(q.att_consts, 16)
        sp.dma_start(sin[:, :], I["c_sin"]).then_inc(q.att_consts, 16)
        sp.dma_start(mem_rows[0][:, :], I["mem_prompt"][0, 0:P, :]).then_inc(q.mem_in, 16)
        sp.dma_start(mem_rows[1][:, :], I["mem_prompt"][0, P:2 * P, :]).then_inc(q.mem_in, 16)
        sp.dma_start(mask[:, :], I["c_mask"]).then_inc(q.att_consts, 16)
        sp.dma_start(mask_first[:, :], I["c_mask_first"]).then_inc(q.att_consts, 16)
        with sp.Fori(0, 2) as i:
            for j in range(2):
                cols(i + (T_ATT // 2 + 2), j, w_in, i * 256 + C_MQ + j * P)
        cols(T_ATT // 2 + 4, 0, w_in, C_SK)
        cols(T_ATT // 2 + 4, 1, w_in, C_SV)
        for h in range(2):
            with sp.Fori(0, 2) as i:
                for j in range(2):
                    load(i + (T_MEM // 2 + 2 * h), j, [(flat(j, s, 512), w_kv[:, bass.ds(i * 4 + 2 * j + s, 1), 512 * h:512 * h + 512]
                                                        .rearrange("p k c -> p (k c)")) for s in range(2)])
        last = gate_loop(T_GATE_B // 2, 16, 4, gate_st2, PS_GATE_B)

        def merge_tile(turn, slot, br, mp):
            dst = w_raw[slot][:, :, :].rearrange("p k c -> p (k c)").rearrange("p (k c) -> p k c", k=4)
            c = bass.ds(mp * 256, 256)
            if br == 0:
                load(turn, slot, [(dst[64 * s:64 * s + 64], w_br_swa[s, :, :, c]) for s in range(2)])
            else:
                w = w_br_mem if br == 1 else w_br_gla
                load(turn, slot, [(dst[:, 2 * s:2 * s + 2], w[:, 2 * s:2 * s + 2, c]) for s in range(2)])

        merge_tile(T_MERGE // 2, 0, 0, 0)
        merge_tile(T_MERGE // 2, 1, 1, 0)
        last(3)
        for s in range(3):
            sp.wait_ge(gate_stored[s], 16 * 24)
        sp.wait_ge(q.staged, NT + 1)
        sp.wait_ge(q.sample_turned, 1)

        for k in range(12):
            for j in range(2):
                if k:
                    sp.wait_ge(q.part_done, 6 * k - 3 + 3 * j)
                sp.dma_start(gate_in[j][:, :], gates[GATE_OF[k % 3] * KD + k // 3 * 2 + j]).then_inc(gate_landed[j], 16)
            if k < 10:
                merge_tile((T_MERGE + k + 2) // 2, k % 2, (k + 2) % 3, (k + 2) // 3)
            else:
                cols(T_WO // 2, k % 2, w_o, (k - 10) * P)

        sp.wait_ge(q.y_mm, 72)
        for b in range(2):
            sp.dma_start(rows[b][:, :], I["x_prompt"][0, b * P:(b + 1) * P, :]).then_inc(rows_landed[b], 16)
        sp.dma_start(ln_g[:, :], I["ln1_g"].to_broadcast([P, D])).then_inc(q.ln_consts, 16)
        sp.dma_start(ln_b[:, :], I["ln1_b"].to_broadcast([P, D])).then_inc(q.ln_consts, 16)
        for k in range(2, KD):
            cols((T_WO + k) // 2, k % 2, w_o, k * P)

        def up(turn, slot, c, half):
            cols(turn, slot, w_up, c * P + half * DFF)

        def down(turn, slot, c):
            load(turn, slot, [(flat(slot, s, 512), w_down[:, bass.ds(c, 1), 512 * s:512 * s + 512].rearrange("p k c -> p (k c)"))
                              for s in range(2)])

        T = T_FFN // 2
        up(T, 0, 0, 0)
        up(T, 1, 0, 1)
        for t in range(2, 9):
            sp.wait_ge(q.x1_turned, t - 1)
            if t < NT:
                sp.dma_start(rows[t % 2][:, :], I["x_prompt"][0, t * P:(t + 1) * P, :]).then_inc(rows_landed[t % 2], 16)
            else:
                sp.dma_start(rows[t % 2][0:DEC, :], I["x_sample"][0]).then_inc(rows_landed[t % 2], 16)

        with sp.Fori(0, NF // 2 - 1) as i:
            for k, half in ((1, 0), (1, 1), (2, 0), (2, 1)):
                up(i * 3 + (T + k), half, i * 2 + k, half)
            for k in range(2):
                down(i * 3 + (T + 3), k, i * 2 + k)
        i = NF // 2 - 1
        up(i * 3 + T + 1, 0, NF - 1, 0)
        up(i * 3 + T + 1, 1, NF - 1, 1)
        down(i * 3 + T + 2, 0, NF - 2)
        down(i * 3 + T + 2, 1, NF - 1)
        sp.wait_ge(q.shifted, 9)
        sp.dma_start(ln_g[:, :], I["ln2_g"].to_broadcast([P, D])).then_inc(q.ln_consts, 16)
        sp.dma_start(ln_b[:, :], I["ln2_b"].to_broadcast([P, D])).then_inc(q.ln_consts, 16)

        for t in range(9):
            sp.wait_ge(q.shifted, 9 + t + 1)
            if t < NT:
                sp.dma_start(O["y_prompt"][0, t * P:(t + 1) * P, :], y_rows[t % 4][:, :]).then_inc(y_stored[t % 4], 16)
            else:
                sp.dma_start(O["y_sample"][0], y_rows[t % 4][0:DEC, :]).then_inc(y_stored[t % 4], 16)
        for r in range(4):
            sp.wait_ge(y_stored[r], 16 * (3 if r == 0 else 2))

    @block.gpsimd
    def _(pool):
        pool.memset(wa2[:, :], 0.0).then_inc(q.zeroed, 1)

        def gla_stage(t):
            c, w = tok(t)
            pool.wait_ge(q.la_mm, t)
            pool.tensor_copy(ga_s[:, 0:w], ga_T[:, bass.ds(c, w)]).then_inc(q.ga_staged, 1)
            pool.wait_ge(q.v_turned, t)
            pool.tensor_copy(v_s[:, :, 0:w], z[:, 8:12, bass.ds(c, w)]).then_inc(q.v_staged, 1)
            pool.wait_ge(q.erec_ready, t + 1)
            pool.wait_ge(q.gla_out, t)
            pool.tensor_tensor(silu[:, :, 0:w], z[:, 12:16, bass.ds(c, w)], er[:, :, 0:w], ALU.mult).then_inc(q.silu_ready, 1)

        pool.wait_ge(q.proj_free, PS_GATE_A)
        gla_stage(0)
        with pool.Fori(1, NT) as t:
            gla_stage(t)
        pool.wait_ge(q.state_end, NT)
        pool.dma_start(O["p_gla"][0, 0].rearrange("h k v -> k h v"), S_a[:, :, :]).then_inc(q.st_state, 16)
        pool.dma_start(S_b[:, :, :], I["state_gla"][0, 0].rearrange("h k v -> k h v")).then_inc(q.state_in, 16)
        gla_stage(NT)
        pool.wait_ge(q.state_mid, NT + 1)
        pool.dma_start(O["s_gla"][0, 0].rearrange("h k v -> k h v"), S_a[:, :, :]).then_inc(q.st_state, 16)

        pool.wait_ge(q.att_consts, 80)
        for k in range(15):
            c = ROPE_CHUNKS[k // 3]
            g0, w = GROUPS[k % 3]
            pool.wait_ge(q.rope_mm, k + 1)
            pool.tensor_tensor(z[:, c, g0:g0 + w], z[:, c, g0:g0 + w], cos[:, g0:g0 + w], ALU.mult).then_inc(q.rope_cos, 1)

        pool.wait_ge(q.proj_free, PS_MEM + 2)
        pool.dma_start(O["p_mem_k"][0, 0].rearrange("(t p) h d -> p t (h d)", p=P), mk_rows[:, :, :]).then_inc(q.st_memk, 16)
        pool.wait_ge(q.proj_free, PS_MEM + 4)
        pool.dma_start(O["p_mem_v"][0, 0].rearrange("(t p) h d -> p t (h d)", p=P), mv[0][:, :, :]).then_inc(q.st_memv, 16)
        pool.dma_start(O["s_swa_k"][0, 0, 0:P - DEC], I["cache_swa_k"][0, 0, DEC:P]).then_inc(q.stored, 16)
        pool.dma_start(O["s_swa_v"][0, 0, 0:P - DEC], I["cache_swa_v"][0, 0, DEC:P]).then_inc(q.stored, 16)

        def att_stage(t, b):
            c, w = tok(t)
            if not (isinstance(t, int) and t < 2):
                pool.wait_ge(q.scores_mm, t * 3 - 3)
                pool.wait_ge(q.vs_turned, t - 1)
            pool.tensor_copy(qs[b][:, :, 0:w], z[:, 0:4, bass.ds(c, w)])
            pool.tensor_copy(mqs[b][:, :, 0:w], z[:, 4:8, bass.ds(c, w)])
            if w == P:
                pool.tensor_copy(ks[b][:, :], kpad[:, bass.ds(c, 2 * P)])
            else:
                pool.tensor_copy(ks_s[:, P:P + w], kpad[:, P + c:P + c + w])
            pool.tensor_copy(vs[b][:, 0:w], z[:, 9, bass.ds(c, w)]).then_inc(q.staged, 1)

        pool.wait_ge(q.rope_done, 15)
        pool.wait_ge(q.proj_free, PS_GATE_B)
        pool.wait_ge(q.mem_lo_done, 2)
        pool.wait_ge(q.proj_done, PS_GATE_B)
        pool.wait_ge(q.mk_ready, 1)
        att_stage(0, 0)
        att_stage(1, 1)
        pool.wait_ge(q.st_memk, 16)
        pool.dma_start(mk_s[:, :, :], I["cache_mem_k"][0, 0].rearrange("(t p) h d -> p t (h d)", p=P)).then_inc(q.sample_in, 16)
        pool.dma_start(k_hist[:, :], I["cache_swa_k"][0, 0].rearrange("t h d -> t (h d)")).then_inc(q.sample_in, 16)
        pool.dma_start(v_hist[:, :], I["cache_swa_v"][0, 0].rearrange("t h d -> t (h d)")).then_inc(q.sample_in, 16)
        pool.dma_start(mv[1][:, :, :], I["cache_mem_v"][0, 0].rearrange("(t p) h d -> p t (h d)", p=P)).then_inc(q.sample_in, 16)
        with pool.Fori(0, NT // 2 - 1) as i:
            for b in range(2):
                att_stage(i * 2 + (2 + b), b)
        att_stage(NT, 0)
        pool.wait_ge(q.proj_done, PS_END)
        pool.wait_ge(q.vt_ready, NT + 1)
        pool.tensor_copy(v_out[:, :], vt[1][:, :])
        pool.tensor_copy(v_out_s[:, :], vt[0][0:DEC, :]).then_inc(q.v_out_ready, 1)
        pool.wait_ge(q.v_out_ready, 1)
        pool.dma_start(O["p_swa_v"][0, 0].rearrange("t h d -> t (h d)"), v_out[:, :]).then_inc(q.stored, 16)
        pool.dma_start(O["s_swa_v"][0, 0, P - DEC:P].rearrange("t h d -> t (h d)"), v_out_s[:, :]).then_inc(q.stored, 16)
        pool.wait_ge(q.k_out_ready, 1)
        pool.dma_start(O["p_swa_k"][0, 0].rearrange("t h d -> t (h d)"), k_out[:, :]).then_inc(q.stored, 16)
        pool.dma_start(O["s_swa_k"][0, 0, P - DEC:P].rearrange("t h d -> t (h d)"), k_out_s[:, :]).then_inc(q.stored, 16)

        def shift(lt, buf, w, consts):
            pool.wait_ge(q.scaled, lt + 1)
            pool.wait_ge(q.ln_consts, consts)
            pool.tensor_tensor(buf[0:w, :], buf[0:w, :], ln_b[0:w, :], ALU.add).then_inc(q.shifted, 1)

        for t in range(9):
            shift(t, rows[t % 2], tok(t)[1], 32)

        hist = prm[:, PHI:PHI + 4 * NF].rearrange("p (r j) -> p r j", r=2)

        def ffn_cols(c, par, first):
            for half in range(2):
                j = c + half * NF
                buf = u[par][half]
                pool.tensor_copy(buf[:, GAP + SEQ:GAP + SAMPLE], hist[:, :, bass.ds(j, 1)].rearrange("p r j -> p (r j)"))\
                    .then_inc(q.u_hist, 1)
                pool.wait_ge(q.up_done, 6 if first and par == 0 else c * 6 + (3 * half + 3))
                pool.tensor_copy(tails[:, 0:2, bass.ds(j, 1)].rearrange("p r j -> p (r j)"), buf[:, SEQ:SEQ + 2])\
                    .then_inc(q.u_tail, 1)
                pool.tensor_copy(tails[:, 2:4, bass.ds(j, 1)].rearrange("p r j -> p (r j)"), buf[:, TT:TT + 2])\
                    .then_inc(q.u_tail, 1)

        pool.wait_ge(q.u_zeroed, 1)
        ffn_cols(0, 0, True)
        ffn_cols(1, 1, True)
        with pool.Fori(0, NF // 2 - 1) as i:
            for b in range(2):
                pool.wait_ge(q.conv_done, i * 4 + 2 * b + 2)
                ffn_cols(i * 2 + (2 + b), b, False)
        for t in range(9):
            shift(9 + t, y_rows[t % 4], tok(t)[1], 64)
        pool.wait_ge(q.tails_ready, 2)
        for s, name in enumerate(("p_ffn_conv", "s_ffn_conv")):
            pool.dma_start(O[name][0, 0].rearrange("r (j p) -> (r j) p", p=P), tails_T[s][:, :]).then_inc(q.stored, 16)
        pool.wait_ge(q.st_state, 32)
        pool.wait_ge(q.st_memk, 16)
        pool.wait_ge(q.st_memv, 16)
        pool.wait_ge(q.stored, 16 * 8)

    @block.tensor
    def _(pe):
        def product(out, hi, lo, b_hi, b_lo, start, stop):
            pe.matmul(out, hi, b_hi, start=start, stop=False)
            pe.matmul(out, hi, b_lo, start=False, stop=False)
            return pe.matmul(out, lo, b_hi, start=False, stop=stop)

        def dense(out, hi, lo, c, w):
            for k in range(KD):
                last = product(out, hi[:, k, :], lo[:, k, :], act_hi[:, k, c:c + w], act_lo[:, k, c:c + w],
                               k == 0, k == KD - 1)
            return last

        def tile_start(turn, slot):
            pe.wait_ge(q.w_split_lo, tile_of(turn, slot) + 1)

        def proj_slice(s, par, slot, gi):
            c, w = GROUPS[gi]
            if not (isinstance(s, int) and s < 2):
                pe.wait_ge(q.proj_free, s - 1)
            dense(bank(par)[:, 0:w], w_hi[slot], w_lo[slot], c, w).then_inc(q.proj_done, 1)

        def proj_tile(turn, slot, s, par):
            tile_start(turn, slot)
            for gi in range(3):
                proj_slice(s + gi, (par + gi) % 2, slot, gi)

        pe.wait_ge(q.consts, 16)
        for t in range(9):
            w = tok(t)[1]
            pe.wait_ge(x_landed[X_GROUP[t]], 16 * X_GROUP.count(X_GROUP[t]))
            if t >= 2:
                pe.wait_ge(q.x_lo_done, t - 1)
            dst = pair8(2 + 2 * (t % 2))
            for k in range(KD):
                last = pe.transpose(dst[:, k, 0:w], x_rows[0:w, t, k * P:(k + 1) * P], ident[0:w, 0:w])
            last.then_inc(q.x_turned, 1)
        pe.wait_ge(q.params, 16 * 7)
        for r, (n, c) in enumerate(((112, 0), (89, 112), (88, 201))):
            last = pe.transpose(bank(6)[:, c:c + n], prow[r][0:n, :], ident[0:n, 0:n])
        last.then_inc(q.prm_turned, 1)

        pe.wait_ge(q.x_lo_done, 9)
        proj_tile(0, 0, 0, 0)
        proj_tile(0, 1, 3, 1)
        with pe.Fori(1, 8) as i:
            proj_tile(i, 0, i * 6, 0)
            proj_tile(i, 1, i * 6 + 3, 1)
        pe.wait_ge(q.wga_ready, 1)
        for gi, (c, w) in enumerate(GROUPS):
            pe.wait_ge(q.proj_free, PS_GA + gi - 1)
            dense(bank(gi % 2)[0:RANK, 0:w], wga_hi, wga_lo, c, w).then_inc(q.proj_done, 1)

        def gla_tile(t, w, s_in, s_out, fill):
            blocks = ((0, 64), (64, 64)) if w == P else ((0, w),)
            pe.wait_ge(q.ga_staged, t + 1)
            pe.matmul(bank(2)[0:w, :], ga_s[:, 0:w], wa2[:, :], start=True, stop=True).then_inc(q.la_mm, 1)
            fill(0)
            pe.wait_ge(q.la_ready, t + 1)
            pe.wait_ge(q.lnms_done, t)
            for h in range(H):
                last = pe.matmul(bank4(3)[:, h, 0:w], la[0:w, h * P:(h + 1) * P], cumsum[0:w, 0:w], start=True, stop=True)
            last.then_inc(q.b_mm, 1)
            fill(1)
            pe.wait_ge(q.v_staged, t + 1)
            pe.wait_ge(q.kttok_ready, t)
            for h in range(H):
                last = pe.transpose(bank4(4)[0:w, h, :], v_s[:, h, 0:w], ident[:, :])
            last.then_inc(q.v_turned, 1)
            fill(2)
            pe.wait_ge(q.qdec_ready, t + 1)
            pe.wait_ge(q.kinv_ready, t + 1)
            pe.wait_ge(q.att_ready, t)
            for h in range(H):
                pe.matmul(bank4(5)[0:w, h, 0:w], k_inv[:, h, 0:w], q_dec[:, h, 0:w], start=True, stop=True)
            pe.wait_ge(q.ktail_ready, t + 1)
            pe.wait_ge(q.vtok_ready, t + 1)
            for h in range(H):
                last = pe.transpose(bank4(4)[0:w, h, :], k_tail[:, h, 0:w], ident[:, :])
            last.then_inc(q.kt_turned, 1)
            fill(3)
            pe.wait_ge(q.att_ready, t + 1)
            pe.wait_ge(q.o_normed, t)
            pe.wait_ge(q.state_end, t)
            if w < P:
                pe.wait_ge(q.state_in, 16)
            pe.wait_ge(q.kttok_ready, t + 1)
            c, n = blocks[0]
            for h in range(H):
                last = pe.matmul(bank4(7)[:, h, :], kt_tok[c:c + n, h, :], v_tok[c:c + n, h, :], start=True, stop=True)
            last.then_inc(q.dsa_mm, 1)
            for h in range(H):
                pe.matmul(bank4(6)[:, h, 0:w], v_tok[0:w, h, :], att[0:w, h, 0:w], start=(h == 0), stop=False,
                          skip_group_check=True)
            for h in range(H):
                last = pe.matmul(bank4(6)[:, h, c:c + n], s_in[:, h, :], q_dec[:, h, c:c + n], start=False,
                                 stop=len(blocks) == 1, skip_group_check=True)
            if len(blocks) == 1:
                last.then_inc(q.o_mm, 1)
            fill(4)
            if len(blocks) == 2:
                c, n = blocks[1]
                pe.wait_ge(q.state_mid, t + 1)
                for h in range(H):
                    last = pe.matmul(bank4(6)[:, h, c:c + n], s_out[:, h, :], q_dec[:, h, c:c + n], start=False,
                                     stop=True, skip_group_check=True)
                last.then_inc(q.o_mm, 1)
                for h in range(H):
                    last = pe.matmul(bank4(7)[:, h, :], kt_tok[c:c + n, h, :], v_tok[c:c + n, h, :], start=True, stop=True)
                last.then_inc(q.dsb_mm, 1)
            fill(5)
            pe.wait_ge(q.osq_ready, t + 1)
            pe.matmul(bank4(3)[:, :, 0:w], ones[:, :], osq4[:, :, 0:w], start=True, stop=True).then_inc(q.rms_mm, 1)

        pe.wait_ge(q.gla_consts, 16 * 5)

        def gate_slice(t, k):
            slot, gi = k // 3, k % 3
            if gi == 0:
                tile_start(t + T_GATE_A // 2, slot)
            proj_slice(t * 6 + (PS_GATE_A + k), (PS_GATE_A + k) % 2, slot, gi)

        gla_tile(0, P, S_a, S_b, lambda k: gate_slice(0, k))
        with pe.Fori(1, NT - 1) as t:
            gla_tile(t, P, S_a, S_b, lambda k: gate_slice(t, k))
        gla_tile(NT - 1, P, S_a, S_b, lambda k: gate_slice(NT - 1, k) if k < 3 else None)
        gla_tile(NT, DEC, S_b, S_a, lambda k: gate_slice(NT - 1, k + 3) if k < 3 else None)

        with pe.Fori(0, 5) as i:
            proj_tile(i + T_ATT // 2, 0, i * 6 + PS_ATT, PS_ATT % 2)
            proj_tile(i + T_ATT // 2, 1, i * 6 + (PS_ATT + 3), (PS_ATT + 3) % 2)

        pe.wait_ge(q.att_consts, 80)
        pe.wait_ge(q.proj_free, PS_MEM)
        for k in range(15):
            c, (g0, w) = ROPE_CHUNKS[k // 3], GROUPS[k % 3]
            if k >= 2:
                pe.wait_ge(q.rope_sin, k - 1)
            pe.matmul(bank(2 + k % 2)[:, 0:w], turn[:, :], z[:, c, g0:g0 + w], start=True, stop=True).then_inc(q.rope_mm, 1)

        for t in range(2):
            pe.wait_ge(q.mem_in, 32)
            dst = pair8(4 + 2 * t)
            for k in range(KD):
                last = pe.transpose(dst[:, k, :], mem_rows[t][:, k * P:(k + 1) * P], ident[:, :])
            last.then_inc(q.mem_turned, 1)
        pe.wait_ge(q.mem_lo_done, 2)
        for h in range(2):
            for k2 in range(4):
                turn_, slot = T_MEM // 2 + 2 * h + k2 // 2, k2 % 2
                tile_start(turn_, slot)
                wh, wl = (x[slot][:, :, :].rearrange("p (k c) m -> p k (c m)", k=2) for x in (w_hi, w_lo))
                for t in range(2):
                    if k2 == 0:
                        pe.wait_ge(q.proj_free, PS_MEM + 2 * h + t - 1)
                    for k in range(2):
                        kk = 2 * k2 + k
                        last = product(bank((PS_MEM + t) % 2), mem_hi[:, kk, t * P:(t + 1) * P], mem_lo[:, kk, t * P:(t + 1) * P],
                                       wh[:, k, :], wl[:, k, :], kk == 0, kk == KD - 1)
                    if k2 == 3:
                        last.then_inc(q.proj_done, 1)
                    elif k2 < 3 and t == 1:
                        last.then_inc(q.mem_used, 1)
            if h == 0:
                pe.wait_ge(q.proj_free, PS_MEM + 2)
                for hh in range(H):
                    for t in range(2):
                        last = pe.transpose(pair8(4)[:, hh * 2 + t, :], mk_rows[:, t, hh * P:(hh + 1) * P], ident[:, :])
                last.then_inc(q.mk_turned, 1)

        def scores(r, b, w, mem, keys, nk):
            for h in range(H):
                out = psum[0:w, 2 + h // 2, (h % 2) * 256:(h % 2) * 256 + nk]
                if r < 2:
                    rows_ = slice(64 * r, 64 * r + 64)
                    last = pe.matmul(out, qs[b][rows_, h, 0:w], keys[rows_, 0:nk], start=True, stop=True)
                else:
                    last = pe.matmul(out, mqs[b][:, h, 0:w], mkT[mem][:, h, :], start=True, stop=True)
            last.then_inc(q.scores_mm, 1)

        def turn_values(t, b, w):
            pe.wait_ge(q.staged, t + 1)
            pe.wait_ge(q.vt_ready, t)
            pe.transpose(bank(7)[0:w, 0:P], vs[b][:, 0:w], ident[:, :]).then_inc(q.vs_turned, 1)

        def turn_probs(k, par, w, widths):
            pe.wait_ge(q.prob_ready, k + 1)
            pe.wait_ge(q.pT_dve, k)
            pe.wait_ge(q.pT_act, k)
            for h in range(H):
                for s, n in enumerate(widths):
                    last = pe.transpose(pair8(4)[0:n, 2 * h + s, 0:w], prob[par][0:w, h, s * P:s * P + n], ident[0:w, 0:w])
            last.then_inc(q.prob_turned, 1)

        def values(k, r, w, pair_, widths):
            pe.wait_ge(q.pT_dve, k + 1)
            pe.wait_ge(q.pT_act, k + 1)
            pe.wait_ge(q.o_evac, k)
            for h in range(H):
                for s, n in enumerate(widths):
                    if r < 2:
                        out, lhs = bank4(6)[64 * r:64 * r + 64, h, 0:w], pair_[s][0:n, 64 * r:64 * r + 64]
                    else:
                        out, lhs = bank4(6)[:, h, 0:w], pair_[:, s, h * P:(h + 1) * P]
                    last = pe.matmul(out, lhs, prob_T[0:n, 2 * h + s, 0:w], start=(s == 0), stop=(s == 1))
            last.then_inc(q.pv_mm, 1)

        def scores_read(k, j, swa):
            if j % 3:
                pe.wait_ge(q.masked, swa)
            else:
                pe.wait_ge(q.exp_done, k)

        def scores_step(k, j, t, swa):
            pe.wait_ge(q.staged, t + 1)
            scores_read(k, j, swa)
            scores(j % 3, j // 3 % 2, P, 0, ks[j // 3 % 2], 2 * P)

        pe.wait_ge(q.mk_ready, 1)
        scores_step(0, 0, 0, 0)
        turn_values(0, 0, P)
        scores_step(1, 1, 0, 1)

        def sample_keys():
            pe.wait_ge(q.sample_in, 64)
            pe.wait_ge(q.pT_dve, 3 * NT - 6)
            pe.wait_ge(q.pT_act, 3 * NT - 6)
            pe.wait_ge(q.vt_ready, NT - 1)
            for hh in range(H):
                for t in range(2):
                    pe.transpose(pair8(4)[:, hh * 2 + t, :], mk_s[:, t, hh * P:(hh + 1) * P], ident[:, :])
            pe.transpose(bank(7)[:, P:2 * P], k_hist[:, :], ident[:, :]).then_inc(q.sample_turned, 1)

        def sample_scores(r):
            scores_read(3 * NT + r, r, 2 * NT + r)
            scores(r, 0, DEC, 1, ks_s, P + DEC if r < 2 else 2 * P)

        def att_steps(i, last):
            if last:
                sample_keys()
            for j in range(6):
                k, b = i * 6 + j, j // 3
                if j % 3 == 0:
                    tile_start(i + T_GATE_B // 2, b)
                proj_slice(i * 6 + (PS_GATE_B + j), (PS_GATE_B + j) % 2, b, j % 3)
                if last and j == 0:
                    pe.wait_ge(q.sample_ready, 1)
                turn_probs(k, j % 2, P, (P, P))
                if last and j >= 4:
                    pe.wait_ge(q.staged, NT + 1)
                    sample_scores(j - 4)
                else:
                    scores_step(k + 2, (j + 2) % 6, i * 2 + (j + 2) // 3, i * 4 + (j + 2) - (j + 2) // 3)
                if j % 3 == 2:
                    turn_values(i * 2 + (b + 1), (b + 1) % 2, DEC if last and j == 5 else P)
                pe.wait_ge(q.vt_ready, i * 2 + (b + 1))
                values(k, j % 3, P, (vt[1 - b], vt[b]) if j % 3 < 2 else mv[0], (P, P))
        att_steps(0, False)
        with pe.Fori(1, NT // 2 - 1) as i:
            att_steps(i, False)
        att_steps(NT // 2 - 1, True)
        for r in range(3):
            k, widths = 3 * NT + r, (P, DEC) if r < 2 else (P, P)
            turn_probs(k, k % 2, DEC, widths)
            if r == 0:
                sample_scores(2)
            pe.wait_ge(q.vt_ready, NT + 1)
            values(k, r, DEC, (v_hist, vt[0]) if r < 2 else mv[1], widths)
        pe.wait_ge(q.pT_dve, 3 * NT + 3)
        pe.wait_ge(q.pT_act, 3 * NT + 3)
        pe.transpose(bank(4)[:, 0:P], ks[1][:, P:2 * P], ident[:, :])
        pe.transpose(bank(4)[0:DEC, P:2 * P], ks_s[:, P:P + DEC], ident[:, :]).then_inc(q.k_turned, 1)

        def merge_tile(turn, slot, k, y0, first):
            tile_start(turn, slot)
            wh, wl = (x[slot][:, :, :].rearrange("p k c -> p (k c)").rearrange("p (k c) -> p k c", k=4) for x in (w_hi, w_lo))
            br = k % 3
            for j in range(2):
                for gi, (c, w) in enumerate(GROUPS):
                    y = k * 6 + 3 * j + gi
                    if first and k < 3 and j == 0:
                        pe.wait_ge(q.ol_split, 3 * br + gi + 1)
                    if not (isinstance(y0, int) and y0 + y < 4):
                        pe.wait_ge(q.part_done, y0 + (y - 3))
                    for kk in range(4):
                        zc = (0, 4, 12)[br] + kk
                        last = product(bank(y % 4)[:, 0:w], wh[:, kk, j * P:(j + 1) * P], wl[:, kk, j * P:(j + 1) * P],
                                       o_hi[:, br * 4 + kk, c:c + w], z_lo[:, zc, c:c + w], kk == 0, kk == 3)
                    last.then_inc(q.y_mm, 1)

        for k in range(6):
            merge_tile((T_MERGE + k) // 2, k % 2, k, 0, True)
        with pe.Fori(1, 2) as i:
            for k in range(6):
                merge_tile(i * 3 + (T_MERGE // 2 + k // 2), k % 2, k, i * 36, False)

        def rows_turn(t, b):
            c, w = tok(t)
            for k in range(KD):
                last = pe.transpose(pair8(b)[0:w, k, :], acc[:, k, c:c + w], ident[:, :])
            last.then_inc(q.r_turned, 1)

        def r1(t):
            pe.wait_ge(q.wo_free, 8 * ((t * P + P > 352) + (t * P + P > 704) + 1))
            pe.wait_ge(q.r_done, t)
            rows_turn(t, 4)

        def x1(t):
            w = tok(t)[1]
            pe.wait_ge(q.shifted, t + 1)
            pe.wait_ge(q.x1_lo_done, t)
            pe.wait_ge(q.x1_acc_done, t)
            for k in range(KD):
                last = pe.transpose(pair8(6)[:, k, 0:w], rows[t % 2][0:w, k * P:(k + 1) * P], ident[0:w, 0:w])
            last.then_inc(q.x1_turned, 1)

        pe.wait_ge(q.mix_ready, 8)
        ln_at = {(1, 1): (r1, 0), (1, 3): (r1, 1), (1, 5): (x1, 0), (2, 1): (r1, 2), (2, 2): (x1, 1), (2, 3): (r1, 3),
                 (2, 4): (x1, 2), (2, 6): (r1, 4), (2, 7): (x1, 3)}
        for gi, (c, w) in enumerate(GROUPS):
            for mm in range(KD):
                y = gi * KD + mm
                if gi == 0:
                    pe.wait_ge(q.w_split_lo, T_WO + mm + 1)
                if y >= 4:
                    pe.wait_ge(q.wo_free, y - 3)
                dense(bank(y % 4)[:, 0:w], wo_hi[:, mm, :, :], wo_lo[:, mm, :, :], c, w).then_inc(q.wo_mm, 1)
                if (gi, mm) in ln_at:
                    step, t = ln_at[gi, mm]
                    step(t)

        HI, LO = (w_hi[0], w_hi[1], w3_hi), (w_lo[0], w_lo[1], w3_lo)

        def up_slice(s, par, ring_slot, gi):
            c, w = GROUPS[gi]
            if not (isinstance(s, int) and s < 4):
                pe.wait_ge(q.up_done, s - 3)
            dense(bank(par)[:, 0:w], HI[ring_slot], LO[ring_slot], c, w).then_inc(q.up_mm, 1)

        def up_tile(turn, slot, ring_slot, s, par):
            tile_start(turn, slot)
            for gi in range(3):
                up_slice(s + gi, (par + gi) % 4, ring_slot, gi)

        def down_tiles(turn, ring0, ring1, s0, chunks, after=None):
            tile_start(turn, 0)
            tile_start(turn, 1)
            pe.wait_ge(q.h_ready, chunks)
            for gi, (c, w) in enumerate(GROUPS):
                for mm in range(KD):
                    y = gi * KD + mm
                    if y >= 4:
                        pe.wait_ge(q.down_free, s0 + (y - 3))
                    out = bank(4 + y % 4)[:, 0:w]
                    product(out, HI[ring0][:, mm, :], LO[ring0][:, mm, :], h_hi[0][:, c:c + w], h_lo[0][:, c:c + w], True, False)
                    product(out, HI[ring1][:, mm, :], LO[ring1][:, mm, :], h_hi[1][:, c:c + w], h_lo[1][:, c:c + w], False, True)\
                        .then_inc(q.down_mm, 1)
                    if after:
                        after(gi, mm)

        T = T_FFN // 2
        tile_start(T, 0)
        tile_start(T, 1)
        steps = [[(r1, 5), (x1, 4)], [(r1, 6)], [(x1, 5), (r1, 7)], [(x1, 6)], [(r1, 8), (x1, 7), (x1, 8)], []]
        for s in range(6):
            for step, t in steps[s]:
                step(t)
            pe.wait_ge(q.x1_lo_done, (3, 6, 9)[s // 2])
            up_slice(s, s % 4, s % 2, s // 2)
        with pe.Fori(0, NF // 2 - 1) as i:
            for k in range(4):
                up_tile(i * 3 + (T + 1 + k // 2), k % 2, (2 + k) % 3, i * 12 + (6 + 3 * k), (6 + 3 * k) % 4)
            down_tiles(i * 3 + (T + 3), 0, 1, i * 24, i * 2 + 2)
        i = NF // 2 - 1
        for k in range(2):
            up_tile(i * 3 + T + 1, k, (2 + 6 * i + k) % 3, i * 12 + 6 + 3 * k, (6 + 3 * k) % 4)

        def r2(t):
            pe.wait_ge(q.down_free, 24 * i + 8 * ((t * P + P > 352) + (t * P + P > 704) + 1))
            if t >= 2:
                pe.wait_ge(q.norm_done, 9 + t - 1)
            else:
                pe.wait_ge(q.up_done, 22 * 6)
            rows_turn(t, 2 * (t % 2))

        ln_at2 = {(1, 1): 0, (1, 5): 1, (2, 2): 2, (2, 6): 3}
        down_tiles(i * 3 + T + 2, (2 + 6 * i + 2) % 3, (2 + 6 * i + 3) % 3, 24 * i, NF,
                   lambda gi, mm: r2(ln_at2[gi, mm]) if (gi, mm) in ln_at2 else None)
        for t in range(4, 9):
            r2(t)
        pe.wait_ge(q.u_tail, 4 * NF)
        for s in range(2):
            last = pe.transpose(bank(4)[0:88, s * P:(s + 1) * P], tails[:, 2 * s:2 * s + 2, :].rearrange("p r j -> p (r j)"), ident[:, :])
        last.then_inc(q.tails_turned, 1)

    @block.scalar
    def _(act):
        def split_hi(turn, slot, dst=None, used=None):
            if used is not None:
                act.wait_ge(*used)
            act.wait_ge(w_landed[slot], (turn + 1) * 32)
            dst = w_hi[slot] if dst is None else dst
            act.activation(dst[:, :, :], w_raw[slot][:, :, :], ACT.Copy).then_inc(q.w_split_hi, 1)

        split_hi(0, 0)
        split_hi(0, 1)
        for t in range(9):
            c, w = tok(t)
            act.wait_ge(q.x_turned, t + 1)
            act.activation(act_hi[:, :, c:c + w], pair8(2 + 2 * (t % 2))[:, :, 0:w], ACT.Copy).then_inc(q.x_hi_done, 1)
        act.wait_ge(q.prm_turned, 1)
        act.activation(prm[:, :], bank(6)[:, 0:NPRM], ACT.Copy).then_inc(q.prm_ready, 1)

        def proj_tile(s, par, chunk):
            for gi, (c, w) in enumerate(GROUPS):
                act.wait_ge(q.proj_done, s + (gi + 1))
                act.activation(z[:, bass.ds(chunk, 1), c:c + w].rearrange("p k c -> p (k c)"), bank((par + gi) % 2)[:, 0:w],
                               ACT.Copy).then_inc(q.proj_free, 1)

        act.wait_ge(q.prm_ready, 1)

        with act.Fori(0, 8) as i:
            for j in range(2):
                proj_tile(i * 6 + 3 * j, j, i * 2 + j)
                split_hi(i + 1, j)
        act.wait_ge(q.gla_consts, 16 * 5)
        act.activation(wga_hi[:, :, :], wga[:, :, :], ACT.Copy).then_inc(q.wga_split_hi, 1)
        for gi, (c, w) in enumerate(GROUPS):
            s = PS_GA + gi
            act.wait_ge(q.proj_done, s + 1)
            act.activation(ga_T[0:RANK, c:c + w], bank(gi % 2)[0:RANK, 0:w], ACT.Copy).then_inc(q.proj_free, 1)

        def gate_out(s, par, gi, staging, stored):
            w = GROUPS[gi][1]
            act.wait_ge(q.proj_done, s + 1)
            if not (isinstance(stored, int) and stored == 0):
                act.wait_ge(gate_stored[gi], stored * 16)
            act.activation(staging[gi][:, 0:w], bank(par)[:, 0:w], ACT.Copy).then_inc(q.proj_free, 1)

        def gla_tile(t, fill):
            c, w = tok(t)
            blocks = w // min(w, BLK)
            bl = w // blocks
            act.wait_ge(q.la_mm, t + 1)
            act.activation(sp_a[0:w, :], bank(2)[0:w, :], ACT.Abs).then_inc(q.abs_done, 1)
            act.wait_ge(q.abs_done, t + 1)
            act.activation(sp_a[0:w, :], sp_a[0:w, :], ACT.Exp, scale=-1.0).then_inc(q.expabs_done, 1)
            act.wait_ge(q.expabs_done, t + 1)
            act.wait_ge(q.gla_out, t)
            act.activation(sp_l[0:w, :], sp_a[0:w, :], ACT.Ln, bias=1.0).then_inc(q.ln1p_done, 1)
            fill(0)
            act.wait_ge(q.b_mm, t + 1)
            act.wait_ge(q.silu_ready, t)
            act.activation(b_s[:, :, 0:w], bank4(3)[:, :, 0:w], ACT.Copy).then_inc(q.b_copied, 1)
            act.activation(e_p[:, :, 0:w], bank4(3)[:, :, 0:w], ACT.Exp).then_inc(q.epos_ready, 1)
            act.activation(e_n[:, :, 0:w], bank4(3)[:, :, 0:w], ACT.Exp, scale=-1.0).then_inc(q.eneg_ready, 1)
            act.wait_ge(q.state_end, t)
            act.activation(decay[:, :, 0:blocks], bank4(3)[:, :, bl - 1:w:bl], ACT.Exp).then_inc(q.decay_ready, 1)
            fill(1)
            act.wait_ge(q.diff_ready, t + 1)
            act.activation(e_t[:, :, 0:w], e_t[:, :, 0:w], ACT.Exp).then_inc(q.etail_ready, 1)
            act.activation(er[:, :, 0:w], z[:, 12:16, bass.ds(c, w)], ACT.Exp, scale=-1.0).then_inc(q.er_ready, 1)
            act.wait_ge(q.v_turned, t + 1)
            act.wait_ge(q.dsb_mm, t)
            act.activation(v_tok[0:w, :, :], bank4(4)[0:w, :, :], ACT.Copy).then_inc(q.vtok_ready, 1)
            fill(2)
            fill(3)
            fill(4)
            act.wait_ge(q.o_mm, t + 1)
            act.activation(osq4[:, :, 0:w], bank4(6)[:, :, 0:w], ACT.Square).then_inc(q.osq_ready, 1)
            fill(5)
            act.wait_ge(q.rms_mm, t + 1)
            act.activation(lnms4[:, :, 0:w], bank4(3)[:, :, 0:w], ACT.Ln, bias=eps[:, 0:1]).then_inc(q.lnms_done, 1)
            act.wait_ge(q.lnms_done, t + 1)
            act.activation(rstd4[:, :, 0:w], lnms4[:, :, 0:w], ACT.Exp, scale=-0.5).then_inc(q.rstd_ready, 1)

        def gate_slice(t, k):
            gate_out(t * 6 + (PS_GATE_A + k), (PS_GATE_A + k) % 2, k % 3, gate_st, t * 2 + k // 3)
            if k % 3 == 2:
                split_hi(t + (T_GATE_A // 2 + 1), k // 3)

        gla_tile(0, lambda k: gate_slice(0, k))
        with act.Fori(1, NT - 1) as t:
            gla_tile(t, lambda k: gate_slice(t, k))
        gla_tile(NT - 1, lambda k: gate_slice(NT - 1, k) if k < 3 else None)
        gla_tile(NT, lambda k: gate_slice(NT - 1, k + 3) if k < 3 else None)

        with act.Fori(0, 5) as i:
            for j in range(2):
                proj_tile(i * 6 + (PS_ATT + 3 * j), (PS_ATT + 3 * j) % 2, i * 2 + j)
                split_hi(i + (T_ATT // 2 + 1), j)

        for t in range(2):
            act.wait_ge(q.mem_turned, t + 1)
            act.activation(mem_hi[:, :, t * P:(t + 1) * P], pair8(4 + 2 * t), ACT.Copy).then_inc(q.mem_hi_done, 1)
        for k in range(8):
            if k % 4 == 3:
                for t in range(2):
                    s = PS_MEM + 2 * (k // 4) + t
                    dst = mk_rows if k < 4 else mv[0]
                    act.wait_ge(q.proj_done, s + 1)
                    act.activation(dst[:, t, :], bank(s % 2), ACT.Copy).then_inc(q.proj_free, 1)
                split_hi((T_MEM + k + 2) // 2, k % 2)
                if k == 3:
                    act.wait_ge(q.mk_turned, 1)
                    act.activation(mkT[0][:, :, :].rearrange("p h (t c) -> p (h t) c", t=2), pair8(4), ACT.Copy).then_inc(q.mk_ready, 1)
            else:
                split_hi((T_MEM + k + 2) // 2, k % 2, used=(q.mem_used, k - k // 4 + 1))

        def exp_unit(k, swa, r, par, w, nk):
            act.wait_ge(q.nbias_done, k + 1)
            for h in range(H):
                src = prob[par][0:w, h, 0:nk] if r < 2 else psum[0:w, 2 + h // 2, (h % 2) * 256:(h % 2) * 256 + nk]
                last = act.activation(prob[par][0:w, h, 0:nk], src, ACT.Exp, bias=nbias[par][0:w, h:h + 1],
                                      scale=SWA_SCALE if r < 2 else MEM_SCALE, accum_out=ssum[par][0:w, h:h + 1])
            last.then_inc(q.exp_done, 1)
            if r < 2:
                act.wait_ge(q.sdif_done, swa + 1)
                act.activation(sexp[par][0:w, :], sdif[par][0:w, :], ACT.Exp).then_inc(q.sexp_done, 1)

        def probs_out(k, w):
            act.wait_ge(q.prob_turned, k + 1)
            act.wait_ge(q.pv_mm, k)
            act.activation(prob_T[:, 4:8, 0:w], pair8(4)[:, 4:8, 0:w], ACT.Copy).then_inc(q.pT_act, 1)

        def values_out(k, r, c, w):
            act.wait_ge(q.pv_mm, k + 1)
            if r < 2:
                dst, src = z[64 * r:64 * r + 64, 0:4, bass.ds(c, w)], bank4(6)[64 * r:64 * r + 64, :, 0:w]
            else:
                dst, src = z[:, 4:8, bass.ds(c, w)], bank4(6)[:, :, 0:w]
            act.activation(dst, src, ACT.Copy).then_inc(q.o_evac, 1)

        def turned_values(t, b, w):
            act.wait_ge(q.vs_turned, t + 1)
            if not (isinstance(t, int) and t < 2):
                act.wait_ge(q.pv_mm, t * 3 - 1)
            act.activation(vt[b][0:w, :], bank(7)[0:w, 0:P], ACT.Copy).then_inc(q.vt_ready, 1)

        turned_values(0, 0, P)
        exp_unit(0, 0, 0, 0, P, 2 * P)
        exp_unit(1, 1, 1, 1, P, 2 * P)

        def att_steps(i, last):
            if last:
                act.wait_ge(q.sample_turned, 1)
                act.activation(mkT[1][:, :, :].rearrange("p h (t c) -> p (h t) c", t=2), pair8(4), ACT.Copy)
                act.activation(ks_s[:, 0:P], bank(7)[:, P:2 * P], ACT.Copy).then_inc(q.sample_ready, 1)
            for j in range(6):
                k, b = i * 6 + j, j // 3
                gate_out(k + PS_GATE_B, (PS_GATE_B + j) % 2, j % 3, gate_st2, i * 2 + (16 + b))
                probs_out(k, P)
                if j % 3 == 2:
                    turned_values(i * 2 + (b + 1), (b + 1) % 2, DEC if last and j == 5 else P)
                c, w = tok(i * 2 + b)
                values_out(k, j % 3, c, w)
                if j % 3 == 2:
                    split_hi(i + (T_GATE_B // 2 + 1), b)
                n = j + 2
                w, nk = (DEC, P + DEC) if last and j >= 4 else (P, 2 * P)
                exp_unit(k + 2, i * 4 + (n - n // 3), n % 3, n % 2, w, nk)
        act.wait_ge(q.rope_done, 15)
        att_steps(0, False)
        with act.Fori(1, NT // 2 - 1) as i:
            att_steps(i, False)
        att_steps(NT // 2 - 1, True)
        for r in range(3):
            k = 3 * NT + r
            probs_out(k, DEC)
            values_out(k, r, SAMPLE, DEC)
            if r == 0:
                exp_unit(k + 2, None, 2, k % 2, DEC, 2 * P)

        act.wait_ge(q.o_evac, 3 * NT + 3)
        act.wait_ge(q.st_memv, 16)
        act.wait_ge(q.v_out_ready, 1)
        for gi in range(3):
            act.wait_ge(gate_stored[gi], 16 * 24)
        for br, zc in enumerate((0, 4, 12)):
            for c, w in GROUPS:
                act.activation(o_hi[:, 4 * br:4 * br + 4, c:c + w], z[:, zc:zc + 4, c:c + w], ACT.Copy).then_inc(q.oh_split, 1)
            if br == 0:
                act.wait_ge(q.k_turned, 1)
                act.activation(k_out[:, :], bank(4)[:, 0:P], ACT.Copy)
                act.activation(k_out_s[:, :], bank(4)[0:DEC, P:2 * P], ACT.Copy).then_inc(q.k_out_ready, 1)

        def merge_tile(i, k):
            for j in range(2):
                act.wait_ge(gate_landed[j], i * 96 + 16 * (k + 1))
                col = PBG + GATE_OF[k % 3] * KD + i * 4 + 2 * (k // 3) + j
                act.activation(gate_in[j][:, :], gate_in[j][:, :], ACT.Sigmoid, bias=prm[:, col:col + 1]).then_inc(q.gate_sig, 1)
                if k % 3 == 0 and (i, k) != (0, 0):
                    mix_out(i * 4 + (2 * (k // 3) - 2 + j))

        def mix_out(mm):
            act.wait_ge(q.acc_ready, mm + 1)
            if isinstance(mm, int) and mm == KD - 1:
                act.wait_ge(q.stored, 16 * 6)
            act.activation(act_hi[:, bass.ds(mm, 1), :], mix_acc[:, bass.ds(mm, 1), :], ACT.Copy).then_inc(q.mix_hi_done, 1)

        for k in range(6):
            merge_tile(0, k)
            split_hi((T_MERGE + k + 2) // 2, k % 2, used=(q.y_mm, 6 * (k + 1)))
        for k in range(6):
            merge_tile(1, k)
            if k < 4:
                split_hi((T_MERGE + k + 8) // 2, k % 2, used=(q.y_mm, 36 + 6 * (k + 1)))
        mix_out(6)
        mix_out(7)

        act.wait_ge(q.y_mm, 72)
        act.wait_ge(q.part_done, 72)
        for k in range(KD):
            act.wait_ge(w_landed[k % 2], ((T_WO + k) // 2 + 1) * 32)
            act.activation(wo_hi[:, k, :, :], w_raw[k % 2][:, :, :], ACT.Copy).then_inc(q.w_split_hi, 1)

        def wo_out(y):
            gi, mm = divmod(y, KD)
            c, w = GROUPS[gi]
            act.wait_ge(q.wo_mm, y + 1)
            act.activation(acc[:, mm, c:c + w], bank(y % 4)[:, 0:w], ACT.Copy).then_inc(q.wo_free, 1)

        def ln_sd_step(t, lt):
            b, w = t % 2, tok(t)[1]
            act.wait_ge(q.aggr_done, lt + 1)
            act.activation(ln_sd[b][0:w, :], ln_mv[b][0:w, 1:2], ACT.Sqrt, bias=eps[0:w, 0:1]).then_inc(q.sd_done, 1)

        def x1_out(t):
            c, w = tok(t)
            act.wait_ge(q.x1_turned, t + 1)
            act.activation(act_hi[:, :, c:c + w], pair8(6)[:, :, 0:w], ACT.Copy)
            act.activation(acc[:, :, c:c + w], pair8(6)[:, :, 0:w], ACT.Copy, scale=ALPHA).then_inc(q.x1_acc_done, 1)

        ln_at = {11: [(ln_sd_step, 0)], 13: [(ln_sd_step, 1)], 15: [(x1_out, 0)], 18: [(ln_sd_step, 2), (x1_out, 1)],
                 20: [(ln_sd_step, 3), (x1_out, 2)], 23: [(ln_sd_step, 4), (x1_out, 3)]}
        for y in range(24):
            wo_out(y)
            for step, t in ln_at.get(y, ()):
                step(t, t) if step is ln_sd_step else step(t)

        HI = (w_hi[0], w_hi[1], w3_hi)

        def up_out(s, par, buf, gi):
            c, w = GROUPS[gi]
            act.wait_ge(q.up_mm, s + 1)
            if gi < 2:
                act.activation(buf[:, GAP + c:GAP + c + w], bank(par)[:, 0:w], ACT.Copy).then_inc(q.up_done, 1)
            else:
                act.activation(buf[:, GAP + c:GAP + SEQ], bank(par)[:, 0:SEQ - c], ACT.Copy)
                act.activation(buf[:, GAP + SAMPLE:GAP + TT], bank(par)[:, SAMPLE - c:TT - c], ACT.Copy).then_inc(q.up_done, 1)

        def gelu(c):
            act.wait_ge(q.conv_done, c * 2 + 1)
            act.activation(conv[0][:, :], conv[0][:, :], ACT.Gelu_apprx_tanh).then_inc(q.gelu_done, 1)

        def h_out(c, b, downs):
            act.wait_ge(q.hmul_done, c + 1)
            if not (isinstance(downs, int) and downs == 0):
                act.wait_ge(q.down_mm, downs)
            act.activation(h_hi[b][:, :], conv[1][:, :], ACT.Copy).then_inc(q.h_hi_done, 1)

        T = T_FFN // 2
        act.wait_ge(q.wo_mm, 24)
        split_hi(T, 0)
        split_hi(T, 1)
        ln_sd_step(5, 5)
        x1_out(4)
        up_out(0, 0, u[0][0], 0)
        ln_sd_step(6, 6)
        up_out(1, 1, u[0][1], 0)
        x1_out(5)
        ln_sd_step(7, 7)
        up_out(2, 2, u[0][0], 1)
        x1_out(6)
        up_out(3, 3, u[0][1], 1)
        ln_sd_step(8, 8)
        x1_out(7)
        x1_out(8)
        up_out(4, 0, u[0][0], 2)
        up_out(5, 1, u[0][1], 2)
        gelu(0)

        def body(i, last):
            turn = i * 3 + (T + 1)
            downs = i * 24

            def split_ring(k):
                split_hi(turn + k // 2, k % 2, HI[(2 + k) % 3])

            if not (isinstance(i, int) and i == 0):
                act.wait_ge(q.down_mm, downs)
            split_ring(1)
            h_out(i * 2, 0, downs)
            split_ring(2)
            for gi in range(3):
                up_out(i * 12 + (6 + gi), (2 + gi) % 4, u[1][0], gi)
            if not last:
                split_ring(3)
            for gi in range(3):
                up_out(i * 12 + (9 + gi), (5 + gi) % 4, u[1][1], gi)
            if last:
                split_ring(3)
                gelu(i * 2 + 1)
                h_out(i * 2 + 1, 1, downs)
                return
            for gi in range(3):
                if gi == 2:
                    gelu(i * 2 + 1)
                if gi == 0:
                    split_ring(4)
                up_out(i * 12 + (12 + gi), (8 + gi) % 4, u[0][0], gi)
            split_ring(5)
            h_out(i * 2 + 1, 1, downs)
            for gi in range(3):
                up_out(i * 12 + (15 + gi), (11 + gi) % 4, u[0][1], gi)
            split_ring(6)
            gelu(i * 2 + 2)

        split_hi(T + 1, 0, HI[2])
        body(0, False)
        with act.Fori(1, NF // 2 - 1) as i:
            body(i, False)
        body(NF // 2 - 1, True)

        act.wait_ge(q.u_tail, 4 * NF)
        for t in range(9):
            w = tok(t)[1]
            ln_sd_step(t, 9 + t)
            act.wait_ge(q.nm_done, t + 1)
            if t >= 4:
                act.wait_ge(y_stored[t % 4], 16 * (t // 4))
            src = psum[0:w, 2 * (t % 2):2 * (t % 2) + 2, :].rearrange("p b c -> p (b c)")
            act.activation(y_rows[t % 4][0:w, :], src, ACT.Identity, bias=ln_nm[t % 2][0:w, 0:1],
                           scale=ln_rs[t % 2][0:w, 0:1]).then_inc(q.norm_done, 1)
        act.wait_ge(q.tails_turned, 1)
        for s in range(2):
            act.activation(tails_T[s][:, :], bank(4)[0:88, s * P:(s + 1) * P], ACT.Copy).then_inc(q.tails_ready, 1)

    @block.vector
    def _(dve):
        def split_lo(turn, slot, src=None, dst=None):
            src = w_hi[slot] if src is None else src
            dst = w_lo[slot] if dst is None else dst
            dve.wait_ge(q.w_split_hi, tile_of(turn, slot) + 1)
            dve.tensor_tensor(dst[:, :, :], w_raw[slot][:, :, :], src[:, :, :].bitcast(F32), ALU.subtract).then_inc(q.w_split_lo, 1)

        dve.memset(eps[:, :], LN_EPS)
        dve.memset(ones[:, :], 1.0 / P)
        dve.memset(S_a[:, :, :], 0.0)
        dve.memset(act_hi[:, :, SEQ:SAMPLE].bitcast(F32), 0.0)
        dve.memset(act_lo[:, :, SEQ:SAMPLE].bitcast(F32), 0.0)
        dve.memset(ga_T[:, :], 0.0).then_inc(q.cleared, 1)
        dve.wait_ge(q.cleared, 1)
        dve.memset(ga_T[32:33, :], 1.0).then_inc(q.cleared, 1)
        split_lo(0, 0)
        split_lo(0, 1)
        for t in range(9):
            c, w = tok(t)
            dve.wait_ge(q.x_hi_done, t + 1)
            dve.tensor_tensor(act_lo[:, :, c:c + w], pair8(2 + 2 * (t % 2))[:, :, 0:w], act_hi[:, :, c:c + w].bitcast(F32),
                              ALU.subtract).then_inc(q.x_lo_done, 1)
        dve.wait_ge(q.params, 16 * 7)
        dve.tensor_scalar(neg_sink[:, :], sink[:, :], -1.0, None, ALU.mult)
        dve.memset(att[:, :, :], 0.0)

        with dve.Fori(0, 8) as i:
            for j in range(2):
                split_lo(i + 1, j)
        dve.wait_ge(q.wga_split_hi, 1)
        dve.tensor_tensor(wga_lo[:, :, :], wga[:, :, :], wga_hi[:, :, :].bitcast(F32), ALU.subtract).then_inc(q.wga_ready, 1)

        def gla_tile(t, split):
            c, w = tok(t)
            blocks = w // min(w, BLK)
            bl = w // blocks
            dve.wait_ge(q.ln1p_done, t + 1)
            dve.wait_ge(q.rstd_ready, t)
            dve.scalar_tensor_tensor(la[0:w, :], bank(2)[0:w, :], 0.0, sp_l[0:w, :], ALU.min, ALU.subtract).then_inc(q.la_ready, 1)
            dve.wait_ge(q.b_copied, t + 1)
            if blocks == 2:
                bb, dd = (x[:, :, :].rearrange("p h (b l) -> p (h b) l", l=bl) for x in (b_s, e_t))
            else:
                bb, dd = b_s[:, :, 0:w], e_t[:, :, 0:w]
            dve.tensor_tensor(dd, bb[:, :, bl - 1:bl].to_broadcast([P, H * blocks, bl]), bb, ALU.subtract).then_inc(q.diff_ready, 1)
            dve.wait_ge(q.epos_ready, t + 1)
            dve.wait_ge(q.o_mm, t)
            dve.scalar_tensor_tensor(q_dec[:, :, 0:w], z[:, 0:4, bass.ds(c, w)], GLA_SCALE, e_p[:, :, 0:w], ALU.mult, ALU.mult)\
                .then_inc(q.qdec_ready, 1)
            dve.wait_ge(q.eneg_ready, t + 1)
            dve.tensor_tensor(k_inv[:, :, 0:w], z[:, 4:8, bass.ds(c, w)], e_n[:, :, 0:w], ALU.mult).then_inc(q.kinv_ready, 1)
            dve.wait_ge(q.etail_ready, t + 1)
            dve.tensor_tensor(k_tail[:, :, 0:w], z[:, 4:8, bass.ds(c, w)], e_t[:, :, 0:w], ALU.mult).then_inc(q.ktail_ready, 1)
            dve.wait_ge(q.er_ready, t + 1)
            dve.tensor_scalar(er[:, :, 0:w], er[:, :, 0:w], 1.0, None, ALU.add).then_inc(q.er1_ready, 1)
            split(0)
            dve.wait_ge(q.kt_turned, t + 1)
            dve.tensor_copy(kt_tok[0:w, :, :], bank4(4)[0:w, :, :]).then_inc(q.kttok_ready, 1)
            dve.copy_predicated(att[0:w, :, 0:w], causal[0:w, 0:w].unsqueeze(1).to_broadcast([w, H, w]), bank4(5)[0:w, :, 0:w])\
                .then_inc(q.att_ready, 1)
            dve.wait_ge(q.er1_ready, t + 1)
            dve.reciprocal(er[:, :, 0:w], er[:, :, 0:w]).then_inc(q.erec_ready, 1)
            s_in, s_mid = (S_a, S_b) if blocks == 2 else (S_b, S_a)
            dve.wait_ge(q.dsa_mm, t + 1)
            dve.wait_ge(q.decay_ready, t + 1)
            if blocks == 1:
                dve.wait_ge(q.st_state, 16)
                dve.wait_ge(q.state_in, 16)
            for h in range(H):
                last = dve.scalar_tensor_tensor(s_mid[:, h, :], s_in[:, h, :], decay[:, h, 0:1], bank4(7)[:, h, :], ALU.mult, ALU.add)
            last.then_inc(q.state_mid, 1)
            split(1)
            if blocks == 2:
                dve.wait_ge(q.dsb_mm, t + 1)
                dve.wait_ge(q.state_mid, t + 1)
                for h in range(H):
                    last = dve.scalar_tensor_tensor(S_a[:, h, :], S_b[:, h, :], decay[:, h, 1:2], bank4(7)[:, h, :], ALU.mult, ALU.add)
                last.then_inc(q.state_end, 1)
            dve.wait_ge(q.rstd_ready, t + 1)
            dve.scalar_tensor_tensor(k_inv[:, :, 0:w], bank4(6)[:, :, 0:w], prm[:, PGN:PGN + 1], rstd4[:, :, 0:w], ALU.mult, ALU.mult)\
                .then_inc(q.o_normed, 1)
            dve.wait_ge(q.o_normed, t + 1)
            dve.wait_ge(q.silu_ready, t + 1)
            dve.tensor_tensor(z[:, 12:16, bass.ds(c, w)], k_inv[:, :, 0:w], silu[:, :, 0:w], ALU.mult).then_inc(q.gla_out, 1)

        dve.wait_ge(q.prm_ready, 1)
        gla_tile(0, lambda j: split_lo(T_GATE_A // 2 + 1, j))
        with dve.Fori(1, NT - 1) as t:
            gla_tile(t, lambda j: split_lo(t + (T_GATE_A // 2 + 1), j))
        gla_tile(NT - 1, lambda j: split_lo(T_ATT // 2, 0) if j == 0 else None)
        gla_tile(NT, lambda j: split_lo(T_ATT // 2, 1) if j == 1 else None)
        dve.memset(kpad[:, 0:P], 0.0)

        with dve.Fori(0, 5) as i:
            for j in range(2):
                split_lo(i + (T_ATT // 2 + 1), j)

        for k in range(15):
            c, (g0, w) = ROPE_CHUNKS[k // 3], GROUPS[k % 3]
            dve.wait_ge(q.rope_mm, k + 1)
            dve.tensor_tensor(rope_t[k % 2][:, 0:w], bank(2 + k % 2)[:, 0:w], sin[:, g0:g0 + w], ALU.mult).then_inc(q.rope_sin, 1)
            dve.wait_ge(q.rope_sin, k + 1)
            dve.wait_ge(q.rope_cos, k + 1)
            dst = z[:, c, g0:g0 + w] if c < 8 else kpad[:, P + g0:P + g0 + w]
            dve.tensor_tensor(dst, z[:, c, g0:g0 + w], rope_t[k % 2][:, 0:w], ALU.add).then_inc(q.rope_done, 1)

        for t in range(2):
            dve.wait_ge(q.mem_hi_done, t + 1)
            dve.tensor_tensor(mem_lo[:, :, t * P:(t + 1) * P], pair8(4 + 2 * t), mem_hi[:, :, t * P:(t + 1) * P].bitcast(F32),
                              ALU.subtract).then_inc(q.mem_lo_done, 1)
        for k in range(8):
            split_lo((T_MEM + k + 2) // 2, k % 2)

        scores4 = psum[:, 2:4, :].rearrange("p b (h c) -> p (b h) c", c=2 * P)

        def max_unit(k, swa, r, par, w, nk, band):
            dve.wait_ge(q.scores_mm, k + 1)
            if r < 2:
                dst = prob[par][0:w, :, 0:nk]
                if band is None:
                    dve.tensor_copy(dst, scores4[0:w, :, 0:nk]).then_inc(q.masked, 1)
                else:
                    dve.tensor_tensor(dst, scores4[0:w, :, 0:nk], band[0:w, :].unsqueeze(1).to_broadcast([w, H, nk]), ALU.add)\
                        .then_inc(q.masked, 1)
                dve.wait_ge(q.masked, swa + 1)
                dve.tensor_reduce(smax[par][0:w, :], dst, AX_X, ALU.max).then_inc(q.max_done, 1)
                dve.wait_ge(q.max_done, k + 1)
                dve.scalar_tensor_tensor(nbias[par][0:w, :], smax[par][0:w, :], -SWA_SCALE, neg_sink[0:w, 4 * r:4 * r + 4],
                                         ALU.mult, ALU.min).then_inc(q.nbias_done, 1)
                dve.wait_ge(q.nbias_done, k + 1)
                dve.tensor_tensor(sdif[par][0:w, :], nbias[par][0:w, :], sink[0:w, 4 * r:4 * r + 4], ALU.add).then_inc(q.sdif_done, 1)
            else:
                dve.tensor_reduce(smax[par][0:w, :], scores4[0:w, :, 0:nk], AX_X, ALU.max).then_inc(q.max_done, 1)
                dve.wait_ge(q.max_done, k + 1)
                dve.tensor_scalar(nbias[par][0:w, :], smax[par][0:w, :], -MEM_SCALE, None, ALU.mult).then_inc(q.nbias_done, 1)

        def normalise(k, swa, r, par, w, nk):
            dve.wait_ge(q.exp_done, k + 1)
            den = ssum[par]
            if r < 2:
                dve.wait_ge(q.sexp_done, swa + 1)
                den = sden[par]
                dve.tensor_tensor(den[0:w, :], ssum[par][0:w, :], sexp[par][0:w, :], ALU.add).then_inc(q.den_done, 1)
                dve.wait_ge(q.den_done, swa + 1)
            dve.reciprocal(srec[par][0:w, :], den[0:w, :]).then_inc(q.rec_done, 1)
            dve.wait_ge(q.rec_done, k + 1)
            for h in range(H):
                last = dve.tensor_scalar(prob[par][0:w, h, 0:nk], prob[par][0:w, h, 0:nk], srec[par][0:w, h:h + 1], None, ALU.mult)
            last.then_inc(q.prob_ready, 1)

        def probs_out(k, w):
            dve.wait_ge(q.prob_turned, k + 1)
            dve.wait_ge(q.pv_mm, k)
            dve.tensor_copy(prob_T[:, 0:4, 0:w], pair8(4)[:, 0:4, 0:w]).then_inc(q.pT_dve, 1)

        dve.wait_ge(q.proj_done, PS_GATE_B)
        dve.wait_ge(q.mk_ready, 1)
        dve.wait_ge(q.st_memk, 16)
        dve.memset(vt[1][:, :], 0.0)
        max_unit(0, 0, 0, 0, P, 2 * P, mask_first)
        max_unit(1, 1, 1, 1, P, 2 * P, mask_first)
        normalise(0, 0, 0, 0, P, 2 * P)

        def att_steps(i, last):
            for j in range(6):
                k = i * 6 + j
                n = j + 1
                w, nk = (DEC, P + DEC) if last and n == 6 else (P, 2 * P)
                normalise(k + 1, i * 4 + (n - n // 3), n % 3, n % 2, w, nk)
                probs_out(k, P)
                n = j + 2
                w, nk = (DEC, P + DEC) if last and n >= 6 else (P, 2 * P)
                max_unit(k + 2, i * 4 + (n - n // 3), n % 3, n % 2, w, nk, None if last and n >= 6 else mask)
                if j % 3 == 2:
                    split_lo(i + (T_GATE_B // 2 + 1), j // 3)
        att_steps(0, False)
        with dve.Fori(1, NT // 2 - 1) as i:
            att_steps(i, False)
        att_steps(NT // 2 - 1, True)
        for r in range(3):
            k = 3 * NT + r
            if r < 2:
                normalise(k + 1, 2 * NT + r + 1, r + 1, (k + 1) % 2, DEC, P + DEC if r == 0 else 2 * P)
            probs_out(k, DEC)
            if r == 0:
                max_unit(k + 2, None, 2, k % 2, DEC, 2 * P, None)

        for br, zc in enumerate((0, 4, 12)):
            for gi, (c, w) in enumerate(GROUPS):
                dve.wait_ge(q.oh_split, 3 * br + gi + 1)
                dve.tensor_tensor(z_lo[:, zc:zc + 4, c:c + w], z[:, zc:zc + 4, c:c + w],
                                  o_hi[:, 4 * br:4 * br + 4, c:c + w].bitcast(F32), ALU.subtract).then_inc(q.ol_split, 1)

        def mix_lo(mm):
            dve.wait_ge(q.mix_hi_done, mm + 1)
            chunk = bass.ds(mm, 1)
            dve.tensor_tensor(act_lo[:, chunk, :], mix_acc[:, chunk, :], act_hi[:, chunk, :].bitcast(F32), ALU.subtract)\
                .then_inc(q.mix_ready, 1)

        def merge_tile(i, k, first):
            pair, br = k // 3, k % 3
            for j in range(2):
                mm = i * 4 + (2 * pair + j)
                dve.wait_ge(q.gate_sig, i * 12 + (2 * k + j + 1))
                for gi, (c, w) in enumerate(GROUPS):
                    y = i * 36 + (6 * k + 3 * j + gi)
                    total = mix_acc[:, bass.ds(mm, 1), c:c + w].rearrange("p k c -> p (k c)")
                    gate = gate_in[j][:, c:c + w]
                    dve.wait_ge(q.y_mm, y + 1)
                    src = bank((6 * k + 3 * j + gi) % 4)[:, 0:w]
                    if br == 0:
                        dve.tensor_tensor(total, src, gate, ALU.mult).then_inc(q.part_done, 1)
                        continue
                    p = part[(3 * j + gi) % 4][:, 0:w]
                    dve.tensor_tensor(p, src, gate, ALU.mult).then_inc(q.part_done, 1)
                    dve.wait_ge(q.part_done, y + 1)
                    adds = i * 20 + 10 * pair
                    if br == 2:
                        dve.wait_ge(q.acc_add, adds + 6)
                    done = dve.tensor_tensor(total, total, p, ALU.add)
                    if br == 2 and gi == 2:
                        done.then_inc(q.acc_ready, 1)
                    else:
                        done.then_inc(q.acc_add, 1)
            if k % 3 == 0 and not (first and k == 0):
                for j in range(2):
                    mix_lo(i * 4 + (2 * pair - 2 + j))

        for k in range(6):
            merge_tile(0, k, True)
            split_lo((T_MERGE + k + 2) // 2, k % 2)
        for k in range(6):
            merge_tile(1, k, False)
            if k < 4:
                split_lo((T_MERGE + k + 8) // 2, k % 2)
        mix_lo(6)
        mix_lo(7)

        for k in range(KD):
            dve.wait_ge(q.w_split_hi, T_WO + k + 1)
            dve.tensor_tensor(wo_lo[:, k, :, :], w_raw[k % 2][:, :, :], wo_hi[:, k, :, :].bitcast(F32), ALU.subtract)\
                .then_inc(q.w_split_lo, 1)

        def stats(lt, b, w, halves):
            for s in range(2):
                last = dve.bn_stats(ln_st[b][0:w, s, :], halves[s])
            last.then_inc(q.stats_done, 1)
            dve.wait_ge(q.stats_done, lt + 1)
            dve.bn_aggr(ln_mv[b][0:w, :], ln_st[b][0:w, :, :]).then_inc(q.aggr_done, 1)

        def inverse_sd(lt, b, w):
            dve.wait_ge(q.sd_done, lt + 1)
            dve.reciprocal(ln_rs[b][0:w, :], ln_sd[b][0:w, :]).then_inc(q.rs_done, 1)
            dve.wait_ge(q.rs_done, lt + 1)

        def gain(lt, buf, w, consts):
            dve.wait_ge(q.norm_done, lt + 1)
            dve.wait_ge(q.ln_consts, consts)
            dve.tensor_tensor(buf[0:w, :], buf[0:w, :], ln_g[0:w, :], ALU.mult).then_inc(q.scaled, 1)

        def ln1(t):
            b, w = t % 2, tok(t)[1]
            buf = rows[b]
            dve.wait_ge(q.r_turned, t + 1)
            dve.wait_ge(rows_landed[b], 16 * (t // 2 + 1))
            mix = psum[0:w, 4:6, :].rearrange("p b c -> p (b c)")
            dve.scalar_tensor_tensor(buf[0:w, :], buf[0:w, :], ALPHA, mix, ALU.mult, ALU.add).then_inc(q.r_done, 1)
            dve.wait_ge(q.r_done, t + 1)
            stats(t, b, w, [buf[0:w, 512 * s:512 * s + 512] for s in range(2)])
            inverse_sd(t, b, w)
            dve.tensor_scalar(buf[0:w, :], buf[0:w, :], ln_mv[b][0:w, 0:1], ln_rs[b][0:w, 0:1], ALU.subtract, ALU.mult)\
                .then_inc(q.norm_done, 1)
            gain(t, buf, w, 32)

        def x1_lo(t):
            c, w = tok(t)
            dve.wait_ge(q.x1_acc_done, t + 1)
            dve.tensor_tensor(act_lo[:, :, c:c + w], pair8(6)[:, :, 0:w], act_hi[:, :, c:c + w].bitcast(F32), ALU.subtract)\
                .then_inc(q.x1_lo_done, 1)

        ln1(0)
        for t in range(1, 5):
            ln1(t)
            x1_lo(t - 1)
        dve.wait_ge(q.wo_mm, 24)
        for par in range(2):
            for half in range(2):
                last = dve.memset(u[par][half][:, 0:GAP], 0.0)
        last.then_inc(q.u_zeroed, 1)
        T = T_FFN // 2
        split_lo(T, 0)
        split_lo(T, 1)
        for t in range(5, 9):
            ln1(t)
            x1_lo(t - 1)
        x1_lo(8)

        HI, LO = (w_hi[0], w_hi[1], w3_hi), (w_lo[0], w_lo[1], w3_lo)

        def conv_op(c, par, op, ups):
            half, tap = divmod(op, 3)
            j = c + half * NF
            buf, dst = u[par][half], conv[half]
            param = lambda at_: prm[:, bass.ds(j + at_, 1)]
            if tap == 0:
                dve.wait_ge(q.up_done, 6 if ups is None else ups + 3 * (half + 1))
                dve.wait_ge(q.u_hist, c * 2 + half + 1)
                if half == 1:
                    dve.wait_ge(q.h_hi_done, c)
                dve.tensor_scalar(dst[:, :], buf[:, GAP:GAP + TT], param(PW2), param(PCB), ALU.mult, ALU.add).then_inc(q.conv_part, 1)
            elif tap == 1:
                dve.wait_ge(q.conv_part, c * 4 + 2 * half + 1)
                dve.scalar_tensor_tensor(dst[:, :], buf[:, 0:TT], param(PW0), dst[:, :], ALU.mult, ALU.add).then_inc(q.conv_part, 1)
            else:
                dve.wait_ge(q.conv_part, c * 4 + 2 * half + 2)
                dve.scalar_tensor_tensor(dst[:, :], buf[:, 1:TT + 1], param(PW1), dst[:, :], ALU.mult, ALU.add)\
                    .then_inc(q.conv_done, 1)

        def h_mul(c):
            dve.wait_ge(q.gelu_done, c + 1)
            dve.wait_ge(q.conv_done, c * 2 + 2)
            dve.tensor_tensor(conv[1][:, :], conv[0][:, :], conv[1][:, :], ALU.mult).then_inc(q.hmul_done, 1)

        def h_low(c, b):
            dve.wait_ge(q.h_hi_done, c + 1)
            dve.tensor_tensor(h_lo[b][:, :], conv[1][:, :], h_hi[b][:, :].bitcast(F32), ALU.subtract).then_inc(q.h_ready, 1)

        for op in range(6):
            conv_op(0, 0, op, None)
        h_mul(0)

        def body(i, last):
            turn = i * 3 + (T + 1)
            ln2_at = {10: (ln2_stats, 0), 12: (ln2_scale, 0), 14: (ln2_stats, 1), 15: (ln2_gain, 0), 16: (ln2_scale, 1),
                      18: (ln2_gain, 1), 19: (ln2_stats, 2), 20: (ln2_scale, 2), 22: (ln2_gain, 2), 23: (ln2_stats, 3)}

            def split_ring(k):
                split_lo(turn + k // 2, k % 2, HI[(2 + k) % 3], LO[(2 + k) % 3])

            split_ring(1)
            h_low(i * 2, 0)
            split_ring(2)
            split_ring(3)
            for op in range(6):
                conv_op(i * 2 + 1, 1, op, i * 12 + 6)
            h_mul(i * 2 + 1)
            if not last:
                split_ring(4)
            h_low(i * 2 + 1, 1)
            if not last:
                split_ring(5)
            dve.wait_ge(q.down_free, i * 24)
            for y in range(24):
                gi, mm = divmod(y, KD)
                c, w = GROUPS[gi]
                dve.wait_ge(q.down_mm, i * 24 + (y + 1))
                dve.tensor_tensor(acc[:, mm, c:c + w], bank(4 + y % 4)[:, 0:w], acc[:, mm, c:c + w], ALU.add).then_inc(q.down_free, 1)
                if not last and y % 3 == 2 and y < 18:
                    conv_op(i * 2 + 2, 0, y // 3, i * 12 + 12)
                if not last and y == 10:
                    split_ring(6)
                if not last and y == 21:
                    h_mul(i * 2 + 2)
                if last and y in ln2_at:
                    step, t = ln2_at[y]
                    step(t)

        def ln2_stats(t):
            b, w = t % 2, tok(t)[1]
            dve.wait_ge(q.r_turned, 9 + t + 1)
            stats(9 + t, b, w, [bank(2 * b + s)[0:w, :] for s in range(2)])

        def ln2_scale(t):
            b, w = t % 2, tok(t)[1]
            inverse_sd(9 + t, b, w)
            dve.tensor_scalar(ln_nm[b][0:w, :], ln_mv[b][0:w, 0:1], ln_rs[b][0:w, 0:1], -1.0, ALU.mult, ALU.mult).then_inc(q.nm_done, 1)

        def ln2_gain(t):
            gain(9 + t, y_rows[t % 4], tok(t)[1], 64)

        dve.wait_ge(q.x1_acc_done, 9)
        split_lo(T + 1, 0, HI[2], LO[2])
        body(0, False)
        with dve.Fori(1, NF // 2 - 1) as i:
            body(i, False)
        body(NF // 2 - 1, True)
        ln2_scale(3)
        ln2_stats(4)
        ln2_gain(3)
        ln2_scale(4)
        for t in range(5, 9):
            ln2_stats(t)
            ln2_gain(t - 1)
            ln2_scale(t)
        ln2_gain(8)


_INS = ("x_prompt", "x_sample", "cache_swa_k", "cache_swa_v", "state_gla", "cache_mem_k", "cache_mem_v", "cache_ffn_conv",
        "mem_prompt", "ln1_g", "ln1_b", "ln2_g", "ln2_b", "w_in", "b_gate", "w_gla_a2", "b_gla_a", "gla_norm_g",
        "swa_sinks", "w_mem_kv", "w_br_gla", "w_br_swa", "w_br_mem", "w_o", "w_up", "conv_w", "conv_b", "w_down")
_OUTS = (("y_prompt", (1, SEQ, D)), ("y_sample", (1, DEC, D)),
         ("p_swa_k", (1, 1, P, 2, 64)), ("p_swa_v", (1, 1, P, 2, 64)), ("p_gla", (1, 1, H, P, P)),
         ("p_mem_k", (1, 1, MEM, H, P)), ("p_mem_v", (1, 1, MEM, H, P)), ("p_ffn_conv", (1, 1, 2, 2 * DFF)),
         ("s_swa_k", (1, 1, P, 2, 64)), ("s_swa_v", (1, 1, P, 2, 64)), ("s_gla", (1, 1, H, P, P)),
         ("s_ffn_conv", (1, 1, 2, 2 * DFF)))


def kernel(**inputs):
    import concourse.bacc as bacc
    from concourse.bass_utils import run_bass_kernel_spmd

    nc = bacc.Bacc("TRN2", target_bir_lowering=False, num_devices=1)
    arrays = {name: np.ascontiguousarray(inputs[name]) for name in _INS}
    arrays.update(shape_constants())
    ins = {name: nc.dram_tensor(f"in_{name}", a.shape, mybir.dt.from_np(a.dtype), kind="ExternalInput").ap()
           for name, a in arrays.items()}
    outs = {name: nc.dram_tensor(f"out_{name}", shape, F32, kind="ExternalOutput").ap() for name, shape in _OUTS}
    build(nc, ins, outs)
    r = run_bass_kernel_spmd(nc, [{f"in_{name}": a for name, a in arrays.items()}], core_ids=[0])
    return tuple(r.results[0][f"out_{name}"] for name, _ in _OUTS)
```
